# Optimizing a Trainium2 kernel written in Bass

```python
import jax, jax.numpy as jnp
from jax import lax
import numpy as np

D_MODEL = 1024
BATCH = 1
SEQ = 128
DEPTH = 2
DEC_BATCH = 1
DEC_SEQ = 512
PAST_LEN = 128

GRID_W = 64
HEAD_DIM = 64
FNET_GROUPS = 8
FNET_GROUP_DIM = 64
FNET_WIDTH = FNET_GROUPS * FNET_GROUP_DIM
CONV_WIDTH = 512
CONV_K = 31
ATTN_HEADS = 8
ATTN_KV_HEADS = 2
ATTN_GROUP = ATTN_HEADS // ATTN_KV_HEADS
ATTN_Q = ATTN_HEADS * HEAD_DIM
ATTN_KV = ATTN_KV_HEADS * HEAD_DIM
WIN_HEADS = 8
WIN_KV_HEADS = 2
WIN_GROUP = WIN_HEADS // WIN_KV_HEADS
WIN_Q = WIN_HEADS * HEAD_DIM
WIN_KV = WIN_KV_HEADS * HEAD_DIM
WINDOW = 128
Q_BLOCK = 128
ROPE_THETA = 10000.0
N_BRANCH = 4
IN_SIZES = (FNET_WIDTH, 2 * CONV_WIDTH, ATTN_Q, ATTN_KV, ATTN_KV, WIN_Q, WIN_KV, WIN_KV, N_BRANCH * D_MODEL)
IN_COLS = sum(IN_SIZES)
N_KEYS = 128
N_EXPERTS = N_KEYS * N_KEYS
PEER_HEADS = 8
PEER_QDIM = 256
PEER_HALF = PEER_QDIM // 2
PEER_TOPK = 16
PEER_CHUNK = 128
EPS = 1e-6
NEG_INF = -1e30

kernel_name = "hybrid_diffusion_prefix_peer_step"

def rmsnorm(x, g):
    xf = x.astype(jnp.float32)
    y = xf * lax.rsqrt(jnp.mean(jnp.square(xf), -1, keepdims=True) + EPS)
    return (y * g.astype(jnp.float32)).astype(x.dtype)

def modulation(cond, w, b):
    ada = jax.nn.silu(cond) @ w + b
    ada = ada.reshape(cond.shape[0], 1, 6, D_MODEL)
    return tuple(ada[:, :, i] for i in range(6))

def axial_rope(s):
    n_rows = s // GRID_W
    row = jnp.repeat(jnp.arange(n_rows), GRID_W).astype(jnp.float32)
    col = jnp.tile(jnp.arange(GRID_W), n_rows).astype(jnp.float32)
    n_f = HEAD_DIM // 4
    inv = 1.0 / (ROPE_THETA ** (jnp.arange(n_f, dtype=jnp.float32) / n_f))
    ang = jnp.concatenate([row[:, None] * inv, col[:, None] * inv], axis=-1)
    return jnp.cos(ang), jnp.sin(ang)

def apply_rope(x, cos, sin):
    half = HEAD_DIM // 2
    shp = (1, x.shape[1]) + (1,) * (x.ndim - 3) + (half,)
    c = cos.reshape(shp).astype(x.dtype)
    s_ = sin.reshape(shp).astype(x.dtype)
    x1, x2 = x[..., :half], x[..., half:]
    return jnp.concatenate([x1 * c - x2 * s_, x1 * s_ + x2 * c], axis=-1)

def block_attention(q, k, v, sink):
    b, sq, kvh, g, hd = q.shape
    nb = sq // Q_BLOCK
    scale = hd ** -0.5
    qb = jnp.moveaxis(q.reshape(b, nb, Q_BLOCK, kvh, g, hd), 1, 0)

    def one(qi):
        s = jnp.einsum("bqhgd,bkhd->bhgqk", qi, k).astype(jnp.float32) * scale
        if sink is not None:
            sc = jnp.broadcast_to(sink.astype(jnp.float32)[None, :, :, None, None], (b, kvh, g, Q_BLOCK, 1))
            p = jax.nn.softmax(jnp.concatenate([s, sc], axis=-1), axis=-1)[..., :-1]
        else:
            p = jax.nn.softmax(s, axis=-1)
        return jnp.einsum("bhgqk,bkhd->bqhgd", p.astype(v.dtype), v)

    o = lax.map(one, qb)
    return jnp.moveaxis(o, 0, 1).reshape(b, sq, kvh, g, hd)

def window_attention(q, k, v, k_ctx, v_ctx, sink):
    b, s, kvh, g, hd = q.shape
    nb = s // Q_BLOCK
    span = 3 * Q_BLOCK
    scale = hd ** -0.5
    pad = ((0, 0), (Q_BLOCK, Q_BLOCK), (0, 0), (0, 0))
    kp = jnp.pad(k, pad)
    vp = jnp.pad(v, pad)
    qb = jnp.moveaxis(q.reshape(b, nb, Q_BLOCK, kvh, g, hd), 1, 0)
    rel = (jnp.arange(span)[None, :] - Q_BLOCK) - jnp.arange(Q_BLOCK)[:, None]
    near = jnp.abs(rel) <= WINDOW
    sink_col = jnp.broadcast_to(sink.astype(jnp.float32)[None, :, :, None, None], (b, kvh, g, Q_BLOCK, 1))

    def one(args):
        qi, blk = args
        start = blk * Q_BLOCK
        kw = lax.dynamic_slice_in_dim(kp, start, span, axis=1)
        vw = lax.dynamic_slice_in_dim(vp, start, span, axis=1)
        kpos = start - Q_BLOCK + jnp.arange(span)
        valid = near & ((kpos >= 0) & (kpos < s))[None, :]
        s_loc = jnp.einsum("bqhgd,bkhd->bhgqk", qi, kw).astype(jnp.float32) * scale
        s_loc = jnp.where(valid, s_loc, NEG_INF)
        s_ctx = jnp.einsum("bqhgd,bkhd->bhgqk", qi, k_ctx).astype(jnp.float32) * scale
        p = jax.nn.softmax(jnp.concatenate([s_loc, s_ctx, sink_col], axis=-1), axis=-1).astype(v.dtype)
        return (jnp.einsum("bhgqk,bkhd->bqhgd", p[..., :span], vw)
                + jnp.einsum("bhgqk,bkhd->bqhgd", p[..., span:-1], v_ctx))

    o = lax.map(one, (qb, jnp.arange(nb)))
    return jnp.moveaxis(o, 0, 1).reshape(b, s, kvh, g, hd)

def fourier_mix(u):
    b, s, _ = u.shape
    ug = u.reshape(b, s, FNET_GROUPS, FNET_GROUP_DIM).astype(jnp.float32)
    f = jnp.fft.fft2(ug, axes=(1, 3), norm="ortho").real
    return f.reshape(b, s, FNET_WIDTH).astype(u.dtype)

def conformer_conv(u, w_dw, b_dw, ln_g, ln_b):
    a, gte = jnp.split(u, 2, axis=-1)
    h = a * jax.nn.sigmoid(gte)
    h = lax.conv_general_dilated(h, w_dw[:, None, :].astype(h.dtype), (1,), [(CONV_K // 2, CONV_K // 2)],
                                 dimension_numbers=("NWC", "WIO", "NWC"),
                                 feature_group_count=CONV_WIDTH) + b_dw
    hf = h.astype(jnp.float32)
    mu = jnp.mean(hf, -1, keepdims=True)
    var = jnp.mean(jnp.square(hf - mu), -1, keepdims=True)
    hn = (hf - mu) * lax.rsqrt(var + EPS) * ln_g.astype(jnp.float32) + ln_b.astype(jnp.float32)
    return jax.nn.silu(hn).astype(u.dtype)

def mixer_block(h, lp, rope, ctx_kv):
    b, s, _ = h.shape
    offs = [int(o) for o in np.cumsum(IN_SIZES)[:-1]]
    f_in, c_in, aq, ak, av, wq, wk, wv, gl = jnp.split(h @ lp["w_in"], offs, axis=-1)
    aq = rmsnorm(aq.reshape(b, s, ATTN_KV_HEADS, ATTN_GROUP, HEAD_DIM), lp["q_norm_g"])
    ak = rmsnorm(ak.reshape(b, s, ATTN_KV_HEADS, HEAD_DIM), lp["k_norm_g"])
    av = av.reshape(b, s, ATTN_KV_HEADS, HEAD_DIM)
    wq = wq.reshape(b, s, WIN_KV_HEADS, WIN_GROUP, HEAD_DIM)
    wk = wk.reshape(b, s, WIN_KV_HEADS, HEAD_DIM)
    wv = wv.reshape(b, s, WIN_KV_HEADS, HEAD_DIM)
    sink = lp["win_sink"].reshape(WIN_KV_HEADS, WIN_GROUP)
    if ctx_kv is None:
        o_attn = block_attention(aq, ak, av, None)
        o_win = block_attention(wq, wk, wv, sink)
        ctx_tensors = (ak, av, wk, wv)
    else:
        cos, sin = rope
        ka_ctx, va_ctx, kw_ctx, vw_ctx = ctx_kv
        aq, ak = apply_rope(aq, cos, sin), apply_rope(ak, cos, sin)
        wq, wk = apply_rope(wq, cos, sin), apply_rope(wk, cos, sin)
        o_attn = block_attention(aq, jnp.concatenate([ak, ka_ctx], axis=1),
                                 jnp.concatenate([av, va_ctx], axis=1), None)
        o_win = window_attention(wq, wk, wv, kw_ctx, vw_ctx, sink)
        ctx_tensors = None
    y_f = fourier_mix(f_in) @ lp["w_fourier_out"]
    y_c = conformer_conv(c_in, lp["conv_dw"], lp["conv_b"], lp["conv_ln_g"], lp["conv_ln_b"]) @ lp["w_conv_out"]
    y_a = o_attn.reshape(b, s, ATTN_Q) @ lp["w_attn_out"]
    y_w = o_win.reshape(b, s, WIN_Q) @ lp["w_win_out"]
    gates = jax.nn.sigmoid(gl.reshape(b, s, N_BRANCH, D_MODEL) + lp["b_gate"])
    merged = gates[:, :, 0] * y_f + gates[:, :, 1] * y_c + gates[:, :, 2] * y_a + gates[:, :, 3] * y_w
    return merged @ lp["w_out"], ctx_tensors

def peer_ffn(h, w_q, subkeys, u_tab, v_tab):
    b, s, d = h.shape
    hc_all = h.reshape(-1, PEER_CHUNK, d)

    def one(hc):
        q = (hc @ w_q).reshape(PEER_CHUNK, PEER_HEADS, 2, PEER_HALF)
        sc = jnp.einsum("chpd,pkd->chpk", q, subkeys).astype(jnp.float32)
        s_half, i_half = lax.top_k(sc, PEER_TOPK)
        cand = s_half[:, :, 0, :, None] + s_half[:, :, 1, None, :]
        cand_idx = i_half[:, :, 0, :, None] * N_KEYS + i_half[:, :, 1, None, :]
        cand = cand.reshape(PEER_CHUNK, PEER_HEADS, PEER_TOPK * PEER_TOPK)
        cand_idx = cand_idx.reshape(PEER_CHUNK, PEER_HEADS, PEER_TOPK * PEER_TOPK)
        top_s, top_pos = lax.top_k(cand, PEER_TOPK)
        eidx = jnp.take_along_axis(cand_idx, top_pos, axis=-1)
        gate = jax.nn.softmax(top_s, axis=-1)
        u = u_tab[eidx]
        v = v_tab[eidx]
        act = jax.nn.gelu(jnp.einsum("chkd,cd->chk", u, hc).astype(jnp.float32))
        return jnp.einsum("chk,chkd->cd", (gate * act).astype(v.dtype), v)

    return lax.map(one, hc_all).reshape(b, s, d)

def trunk_layer(x, mod, lp, rope, ctx_kv):
    sh1, sc1, g1, sh2, sc2, g2 = mod
    h = rmsnorm(x, lp["norm1_g"]) * (1 + sc1) + sh1
    mix, ctx_tensors = mixer_block(h, lp, rope, ctx_kv)
    x = x + g1 * mix
    h = rmsnorm(x, lp["norm2_g"]) * (1 + sc2) + sh2
    x = x + g2 * peer_ffn(h, lp["w_peer_q"], lp["peer_subkeys"], lp["peer_u"], lp["peer_v"])
    return x, ctx_tensors

def setup_inputs(seed: int = 0) -> dict:
    key = jax.random.key(seed)
    ks = iter(jax.random.split(key, 40))
    f32 = jnp.float32

    def nrm(shape, scale):
        return jax.random.normal(next(ks), shape, f32) * scale

    def gain(shape):
        return 1.0 + nrm(shape, 0.02)

    kv_shape = (DEC_BATCH, DEPTH, PAST_LEN, ATTN_KV_HEADS, HEAD_DIM)
    wkv_shape = (DEC_BATCH, DEPTH, PAST_LEN, WIN_KV_HEADS, HEAD_DIM)
    return {
        "x_prompt": nrm((BATCH, SEQ, D_MODEL), 1.0),
        "x_sample": nrm((DEC_BATCH, DEC_SEQ, D_MODEL), 1.0),
        "cache_attn_k": nrm(kv_shape, 1.0),
        "cache_attn_v": nrm(kv_shape, 1.0),
        "cache_win_k": nrm(wkv_shape, 1.0),
        "cache_win_v": nrm(wkv_shape, 1.0),
        "c": nrm((DEC_BATCH, D_MODEL), 1.0),
        "c_ctx": nrm((D_MODEL,), 1.0),
        "norm1_g": gain((DEPTH, D_MODEL)),
        "norm2_g": gain((DEPTH, D_MODEL)),
        "w_ada": nrm((DEPTH, D_MODEL, 6 * D_MODEL), 0.5 * D_MODEL ** -0.5),
        "b_ada": nrm((DEPTH, 6 * D_MODEL), 0.02),
        "w_in": nrm((DEPTH, D_MODEL, IN_COLS), D_MODEL ** -0.5),
        "b_gate": nrm((DEPTH, N_BRANCH, D_MODEL), 0.02),
        "w_fourier_out": nrm((DEPTH, FNET_WIDTH, D_MODEL), FNET_WIDTH ** -0.5),
        "conv_dw": nrm((DEPTH, CONV_K, CONV_WIDTH), CONV_K ** -0.5),
        "conv_b": nrm((DEPTH, CONV_WIDTH), 0.02),
        "conv_ln_g": gain((DEPTH, CONV_WIDTH)),
        "conv_ln_b": nrm((DEPTH, CONV_WIDTH), 0.02),
        "w_conv_out": nrm((DEPTH, CONV_WIDTH, D_MODEL), CONV_WIDTH ** -0.5),
        "q_norm_g": gain((DEPTH, HEAD_DIM)),
        "k_norm_g": gain((DEPTH, HEAD_DIM)),
        "w_attn_out": nrm((DEPTH, ATTN_Q, D_MODEL), ATTN_Q ** -0.5),
        "win_sink": nrm((DEPTH, WIN_HEADS), 1.0),
        "w_win_out": nrm((DEPTH, WIN_Q, D_MODEL), WIN_Q ** -0.5),
        "w_out": nrm((DEPTH, D_MODEL, D_MODEL), D_MODEL ** -0.5),
        "w_peer_q": nrm((DEPTH, D_MODEL, PEER_HEADS * PEER_QDIM), D_MODEL ** -0.5),
        "peer_subkeys": nrm((DEPTH, 2, N_KEYS, PEER_HALF), PEER_HALF ** -0.5),
        "peer_u": nrm((DEPTH, N_EXPERTS, D_MODEL), D_MODEL ** -0.5),
        "peer_v": nrm((DEPTH, N_EXPERTS, D_MODEL), PEER_HEADS ** -0.5),
        "final_norm_g": gain((D_MODEL,)),
    }

def reference(x_prompt, x_sample, cache_attn_k, cache_attn_v, cache_win_k, cache_win_v, c, c_ctx,
              norm1_g, norm2_g, w_ada, b_ada, w_in, b_gate, w_fourier_out, conv_dw, conv_b,
              conv_ln_g, conv_ln_b, w_conv_out, q_norm_g, k_norm_g, w_attn_out, win_sink, w_win_out,
              w_out, w_peer_q, peer_subkeys, peer_u, peer_v, final_norm_g):
    rope = axial_rope(x_sample.shape[1])
    xp, xs = x_prompt, x_sample
    ctx_out = []
    for l in range(DEPTH):
        lp = {
            "norm1_g": norm1_g[l], "norm2_g": norm2_g[l], "w_in": w_in[l], "b_gate": b_gate[l],
            "w_fourier_out": w_fourier_out[l], "conv_dw": conv_dw[l], "conv_b": conv_b[l],
            "conv_ln_g": conv_ln_g[l], "conv_ln_b": conv_ln_b[l], "w_conv_out": w_conv_out[l],
            "q_norm_g": q_norm_g[l], "k_norm_g": k_norm_g[l], "w_attn_out": w_attn_out[l],
            "win_sink": win_sink[l], "w_win_out": w_win_out[l], "w_out": w_out[l],
            "w_peer_q": w_peer_q[l], "peer_subkeys": peer_subkeys[l], "peer_u": peer_u[l], "peer_v": peer_v[l],
        }
        mod_ctx = modulation(c_ctx[None, :], w_ada[l], b_ada[l])
        xp, ctx_t = trunk_layer(xp, mod_ctx, lp, None, None)
        ctx_out.append(ctx_t)
        mod_lat = modulation(c, w_ada[l], b_ada[l])
        cached = (cache_attn_k[:, l], cache_attn_v[:, l], cache_win_k[:, l], cache_win_v[:, l])
        xs, _ = trunk_layer(xs, mod_lat, lp, rope, cached)
    y_prompt = rmsnorm(xp, final_norm_g)
    y_sample = rmsnorm(xs, final_norm_g)
    new_attn_k = jnp.stack([t[0] for t in ctx_out], axis=1)
    new_attn_v = jnp.stack([t[1] for t in ctx_out], axis=1)
    new_win_k = jnp.stack([t[2] for t in ctx_out], axis=1)
    new_win_v = jnp.stack([t[3] for t in ctx_out], axis=1)
    return (y_prompt, y_sample, new_attn_k, new_attn_v, new_win_k, new_win_v)


_drawn_inputs = setup_inputs


def setup_inputs(seed=0):
    import zlib

    import numpy as np

    out = dict(_drawn_inputs(seed))
    spreads = {}
    factors = {'cache_attn_k': 7.254,
     'cache_attn_v': 6.323,
     'cache_win_k': 4.402,
     'cache_win_v': 3.799,
     'norm1_g': 2.869,
     'norm2_g': 4.846,
     'b_gate': 8.0,
     'conv_b': 7.992,
     'conv_ln_g': 8.0,
     'conv_ln_b': 8.0,
     'q_norm_g': 8.0,
     'k_norm_g': 2.809,
     'win_sink': 8.0,
     'final_norm_g': 2.767}
    for name, (base, spread) in spreads.items():
        noise = np.random.default_rng([zlib.crc32(name.encode()), seed]).standard_normal(out[name].shape)
        drawn = base * np.exp(spread * noise) if base else spread * noise
        out[name] = __import__('jax').numpy.asarray(drawn.astype(out[name].dtype))
    for name, factor in factors.items():
        out[name] = (out[name] * factor).astype(out[name].dtype)
    return out
```

```python
from contextlib import ExitStack

import numpy as np
import concourse.bass as bass
from concourse import mybir

F32 = mybir.dt.float32
I32 = mybir.dt.int32
U32 = mybir.dt.uint32
ALU = mybir.AluOpType
ACT = mybir.ActivationFunctionType
AX = mybir.AxisListType

P = 128
D = 1024
DEPTH = 2
KD = D // P
TILES = 5
TOK = TILES * P
LAT = TOK - P
HALF = TOK // 2
HEADS, KVH, HD = 8, 2, 64
GROUP = HEADS // KVH
UNITS = 2 * HEADS
TAPS = 31
PAD = TAPS // 2
CONV = 512
CJ = CONV // P
SPAN = P + 2 * PAD + LAT
CPAD = SPAN + 2 * PAD
EXPERTS = 16384
PH = 8
TOPK = 16
SLOTS = PH * TOPK
EPS = 1e-6
SCALE = HD ** -0.5
NEG = -1e30 / SCALE

N_MOD, N_CP, N_QP, N_MG, N_OP, N_PQ = 24, 4, 8, 32, 4, 8
AT_CP = N_MOD
AT_QP = AT_CP + N_CP
AT_MG = AT_QP + N_QP
AT_OP = AT_MG + N_MG
AT_PQ = AT_OP + N_OP
LOADS = AT_PQ + N_PQ
WS = 4
SLOT_W = 2048

RING = 16
GROUPS = SLOTS // RING

PP = {}
_o = 0
for _n, _w in (("n1", KD), ("n2", KD), ("bada", 48), ("bg", 32), ("cw", CJ * TAPS), ("cb", CJ), ("lg", CJ), ("lb", CJ)):
    PP[_n] = (_o, _w)
    _o += _w
PPW = _o


class Sig:

    def __init__(self, sem, per, first):
        self.sem, self.per, self.first = sem, per, first

    def at(self, layer, n):
        return layer * self.per + (n + self.first)


def program(nc, ws, cst, tabs, masks, ppd, cvec, rowd, fing, skd, kcd, vcd, tables_u, tables_v, xin,
            y_out, nk_out):
    with ExitStack() as ctx:
        def sb(name, shape, dt=F32):
            return ctx.enter_context(nc.sbuf_tensor(name, shape, dt))

        def sig(name, per=1, first=0):
            return Sig(ctx.enter_context(nc.semaphore(name)), per, first)

        x = sb("x", [P, TILES, D])
        hT = sb("hT", [P, KD, TOK])
        A = sb("A", [P, 2560 + 1792 + 6400])
        Fin = A[:, 0:2560].rearrange("p (t n) -> p t n", t=TILES)
        V = A[:, 2560:4352].rearrange("p (b n) -> p b n", b=7)
        TM = A[:, 4352:10752].rearrange("p (t n) -> p t n", t=TILES)
        SC = A[:, 0:10240].rearrange("p (t h k) -> p t h k", t=TILES, h=UNITS)
        M = sb("M", [P, TILES * D])
        convh = M[:, 0:CJ * CPAD].rearrange("p (j n) -> p j n", j=CJ)
        SQ = M[:, 0:CJ * SPAN].rearrange("p (j n) -> p j n", j=CJ)
        G = M[:, 2880:4160].rearrange("p (c n) -> p c n", c=2)
        RSTD = M[:, 4192:4192 + SPAN]
        Pb = [M[:, i * 640:(i + 1) * 640] for i in range(2)]
        PT = [M[:, 1280 + i * 640:1280 + (i + 1) * 640] for i in range(2)]
        MK = M[:, 2560:3584]
        QO = M[:, 3584:4608]
        mT = M[:, :].rearrange("p (k n) -> p k n", k=KD)
        h2 = M[:, :].rearrange("p (t n) -> p t n", t=TILES)
        B = sb("B", [P, 10240 + WS * SLOT_W])
        BR = B[:, 0:10240].rearrange("p (b j n) -> p b j n", b=4, j=CJ)
        YC = B[:, 5120:5120 + CJ * SPAN].rearrange("p (j n) -> p j n", j=CJ)
        Wt = [B[:, 10240 + s * SLOT_W:10240 + (s + 1) * SLOT_W] for s in range(WS)]
        XS = B[:, 0:1024]
        JX = B[:, 1024:2048]
        QS = [B[:, 2048 + i * 640:2048 + (i + 1) * 640] for i in range(2)]
        ring = [B[:, i * 1024:(i + 1) * 1024] for i in range(RING)]
        junk = [B[:, (RING + i) * 1024:(RING + i + 1) * 1024] for i in range(2)]
        EQ = B[:, RING * 1024:(RING + 2) * 1024].rearrange("p (h k a) -> p h k a", h=PH, k=TOPK)
        R = sb("R", [P, 5376])
        CS = R[:, 0:4096].rearrange("p (c t n) -> p c t n", c=2, t=4)
        C1, S1 = R[:, 4096:4224], R[:, 4224:4352]
        qT = R[0:64, 0:2048].rearrange("p (u n) -> p u n", u=UNITS)
        kTa = R[0:64, 2048:3584].rearrange("p (v n) -> p v n", v=KVH)
        kTw = R[0:64, 3584:5376].rearrange("p (v n) -> p v n", v=KVH)
        grow = R[:, 0:4096].rearrange("p (v s n) -> p v s n", v=2, s=2)
        EI = R[:, 4096:4096 + TILES * SLOTS].bitcast(I32)
        GT = R[:, 4736:4736 + TILES * SLOTS]
        T = sb("T", [P, 640])
        SG = [TM[:, 0, 0:640], TM[:, 0, 640:1280]]
        PR = TM[:, 1, 0:640]
        hf = hT[:, :, :].rearrange("p k n -> p (k n)")
        acc = [hf[:, 0:1024], hf[:, 1024:2048]]
        cand = hf[:, 2048:4096].rearrange("p (h c) -> p h c", h=PH)
        S16 = hf[:, 4096:4352].rearrange("p (u k) -> p u k", u=UNITS)
        I16 = hf[:, 4352:4608].bitcast(U32).rearrange("p (u k) -> p u k", u=UNITS)
        F16 = hf[:, 4608:4864].rearrange("p (u k) -> p u k", u=UNITS)
        TS = hf[:, 4864:4992].rearrange("p (h k) -> p h k", h=PH)
        TP = hf[:, 4992:5120].bitcast(U32).rearrange("p (h k) -> p h k", h=PH)
        topw = T[:, 0:512].rearrange("p (i n) -> p i n", i=4)
        dots = T[:, 512:640]
        st_idx = [sb(f"st_idx{i}", [P, RING], I32) for i in range(2)]
        cs = sb("cs", [P, 4, P])
        ident, onesD, BC, BSn = [cs[:, i, :] for i in range(4)]
        rope = sb("rope", [P, 2, 4, HD])
        io = sb("io", [P, 2 * TOPK + DEPTH])
        pp = sb("pp", [P, DEPTH, PPW])
        cT = sb("cT", [P, KD, 2])
        row = sb("row", [P, DEPTH, 2 * HD + HEADS])
        nsink = sb("nsink", [P, HEADS])
        skT = sb("skT", [P, 2, P])
        wgt = skT[:, 0, :]
        adaT = sb("adaT", [P, 48, 2])
        aff = sb("aff", [P, TILES, 4, KD])
        s1 = sb("s1", [P, 16])
        sm = sb("sm", [P, 8, 2])
        nrm = sb("nrm", [P, 3, 10])

        ps = ctx.enter_context(nc.psum_tensor("ps", [P, 8, 512], F32))

        cst_in = sig("cst_in")
        layer_done = sig("layer_done", 1, 1)
        w_in = [sig(f"w_in{s}", 16 * LOADS // WS) for s in range(WS)]
        w_used = sig("w_used", LOADS, WS)
        silu_c = sig("silu_c")
        mod_ev = sig("mod_ev", N_MOD, WS)
        aff_ok = sig("aff_ok", 1)
        n_ssq = sig("n_ssq", 2 * TILES)
        n_sq = sig("n_sq", 2 * TILES)
        n_xs = sig("n_xs", 2 * TILES)
        n_tp = sig("n_tp", 2 * TILES)
        n_ht = sig("n_ht", 2 * TILES, 1)
        pads = sig("pads", 2)
        cp_sg = sig("cp_sg", CJ)
        cp_ev = sig("cp_ev", CJ, 2)
        qp_ps = sig("qp_ps", N_QP * (TILES - 1))
        qp_ev = sig("qp_ev", N_QP * TILES, 4)
        tab_in = sig("tab_in", 16)
        fo_ps = sig("fo_ps", CJ)
        fo_g = sig("fo_g", CJ, 1)
        fo_ops = sig("fo_ops", CJ)
        fo_o = sig("fo_o", CJ, 1)
        cv_y = sig("cv_y", 1)
        ln_mp = sig("ln_mp", 1)
        ln_d = sig("ln_d", 1)
        ln_sq = sig("ln_sq", 1)
        ln_vp = sig("ln_vp", 1)
        ln_v = sig("ln_v", 1)
        ln_sr = sig("ln_sr", 1)
        ln_n = sig("ln_n", 1)
        ln_o = sig("ln_o", 1)
        kq_s = sig("kq_s", TILES)
        kq_r = sig("kq_r", TILES)
        kq_ok = sig("kq_ok", 1)
        kt_ps = sig("kt_ps", 1)
        kt_ev = sig("kt_ev", 1)
        kv_in = sig("kv_in", 16 * 4)
        qs_ok = sig("qs_ok", TILES)
        qt_ps = sig("qt_ps", TILES)
        qt_a = sig("qt_a", TILES)
        qt_d = sig("qt_d", TILES)
        a_s = sig("a_s", UNITS * TILES)
        a_m = sig("a_m", UNITS * TILES)
        a_exp = sig("a_exp", UNITS * TILES, 2)
        a_t = sig("a_t", UNITS * TILES)
        a_pa = sig("a_pa", UNITS * TILES, 1)
        a_pd = sig("a_pd", UNITS * TILES, 1)
        a_o = sig("a_o", UNITS * TILES)
        a_on = sig("a_on", UNITS * TILES, 2)
        ot_ps = sig("ot_ps", TILES)
        ot_ev = sig("ot_ev", TILES, 1)
        rw_dg = sig("rw_dg", 8)
        rw_ps = sig("rw_ps", 8)
        rw_ev = sig("rw_ev", 8, 2)
        mg_g = sig("mg_g", N_MG)
        mg_sg = sig("mg_sg", N_MG)
        mg_ev = sig("mg_ev", N_MG, 2)
        mg_m = sig("mg_m", KD)
        op_ps = sig("op_ps", TILES - 1)
        op_x = sig("op_x", TILES)
        h2_ps = sig("h2_ps", TILES)
        h2_ev = sig("h2_ev", TILES)
        sk_in = sig("sk_in", 16)
        pq_ps = sig("pq_ps", UNITS // 2)
        pq_q = sig("pq_q", UNITS)
        pq_sp = sig("pq_sp", UNITS)
        pq_s = sig("pq_s", UNITS, 2)
        tk_d = sig("tk_d", TILES)
        tk_e = sig("tk_e", TILES)
        ei_ok = sig("ei_ok", TILES)
        st_ok = sig("st_ok", TILES * 2 * GROUPS)
        got = [sig(f"got{b}", 16 * TILES * 2 * GROUPS) for b in range(RING)]
        used = sig("used", TILES * 2 * SLOTS, RING)
        pool_go = sig("pool_go")
        pe_go = sig("pe_go")
        dve_go = sig("dve_go")
        u_done = sig("u_done", TILES)
        u_act = sig("u_act", TILES)
        nk_done = sig("nk_done", 16 * 4)
        f_g = sig("f_g")
        f_ss = sig("f_ss")
        f_sq = sig("f_sq")
        f_y = sig("f_y")
        out_done = sig("out_done")

        block = ctx.enter_context(nc.Block())

        @block.sync
        def _(sp):
            for dst, src in ((x[:, :, :], xin.rearrange("(t p) n -> p t n", p=P)),
                             (cs[:, :, :], cst[:, 0:512].rearrange("p (c n) -> p c n", c=4)),
                             (rope[:, :, :, :], cst[:, 512:1024].rearrange("p (c t n) -> p c t n", c=2, t=4)),
                             (io[:, :], cst[:, 1024:1024 + 2 * TOPK + DEPTH]),
                             (pp[:, :, :], ppd.rearrange("p (l n) -> p l n", l=DEPTH)),
                             (cT[:, :, :], cvec.rearrange("p (k s) -> p k s", k=KD)),
                             (row[:, :, :], rowd.partition_broadcast(P))):
                sp.dma_start(dst, src).then_inc(cst_in.sem, 16)
            with sp.Fori(0, DEPTH) as l:
                sp.wait_ge(layer_done.sem, layer_done.at(l, 0))
                sp.dma_start(R[:, 0:4352], tabs[:, :]).then_inc(tab_in.sem, 16)
                sp.dma_start(skT[:, :, :], skd[bass.ds(l * P, P), :].rearrange("p (c n) -> p c n", c=2))\
                    .then_inc(sk_in.sem, 16)

                def load(n, s, width):
                    sp.wait_ge(w_used.sem, w_used.at(l, n + 1 - WS))
                    sp.dma_start(Wt[s][:, 0:width], ws[bass.ds((l * LOADS + n) * P, P), 0:width])\
                        .then_inc(w_in[s].sem, 16)

                with sp.Fori(0, AT_MG // WS) as q:
                    for s in range(WS):
                        load(q * WS + s, s, SLOT_W)
                sp.wait_ge(fo_ops.sem, fo_ops.at(l, CJ))
                sp.wait_ge(ln_o.sem, ln_o.at(l, 1))
                sp.dma_start(MK, masks[:, :]).then_inc(kv_in.sem, 16)
                sp.dma_start(kTa[:, :, 4 * P:5 * P], kcd[bass.ds(l * 2 * HD, HD), :]
                             .rearrange("p (v n) -> p v n", v=KVH)).then_inc(kv_in.sem, 16)
                sp.dma_start(kTw[:, :, 6 * P:7 * P], kcd[bass.ds(l * 2 * HD + HD, HD), :]
                             .rearrange("p (v n) -> p v n", v=KVH)).then_inc(kv_in.sem, 16)
                sp.dma_start(V[:, 6, :], vcd[bass.ds(l * P, P), :]).then_inc(kv_in.sem, 16)
                sp.wait_ge(kq_ok.sem, kq_ok.at(l, 1))
                for i, src in enumerate((TM[:, 0, 512:640], V[:, 0, 0:128], TM[:, 0, 1152:1280], V[:, 0, 128:256])):
                    sp.dma_start(nk_out[bass.ds((l + i * DEPTH) * P, P), :], src).then_inc(nk_done.sem, 16)
                with sp.Fori(AT_MG // WS, AT_OP // WS) as q:
                    for s in range(WS):
                        load(q * WS + s, s, 12 * P)
                with sp.Fori(AT_OP // WS, LOADS // WS) as q:
                    for s in range(WS):
                        load(q * WS + s, s, SLOT_W)
            sp.wait_ge(layer_done.sem, DEPTH + 1)
            sp.dma_start(R[:, 0:D], fing.partition_broadcast(P)).then_inc(f_g.sem, 16)
            sp.wait_ge(f_y.sem, TILES)
            sp.dma_start(y_out.rearrange("(t p) n -> p t n", p=P), h2).then_inc(out_done.sem, 16)
            sp.wait_ge(out_done.sem, 16)
            sp.wait_ge(nk_done.sem, 64 * DEPTH)

        @block.gpsimd
        def _(pool):
            with pool.Fori(0, DEPTH) as l:
                pool.wait_ge(layer_done.sem, layer_done.at(l, 0))
                pool.sem_inc(pool_go.sem, 1)
                pool.memset(convh, 0.0)
                pool.memset(V[:, 5, :], 0.0).then_inc(pads.sem, 1)
                pool.wait_ge(fo_ops.sem, fo_ops.at(l, CJ))
                pool.sem_inc(pool_go.sem, 1)
                pool.memset(kTw[:, :, 5 * P:6 * P], 0.0).then_inc(pads.sem, 1)
                with pool.Fori(0, TILES) as t:
                    for uv in range(2):
                        table = (tables_u, tables_v)[uv]
                        with pool.Fori(0, GROUPS // 2) as q:
                            for half in range(2):
                                m = (t * 2 + uv) * GROUPS + q * 2 + half
                                pool.wait_ge(st_ok.sem, st_ok.at(l, m + 1))
                                pool.sem_inc(pool_go.sem, 1)
                                for b in range(RING):
                                    pool.wait_ge(used.sem, used.at(l, m * RING + b + 1 - RING))
                                    pool.sem_inc(pool_go.sem, 1)
                                    pool.indirect_dma_start(
                                        out=ring[b], out_offset=None, in_=table[:, :],
                                        in_offset=bass.IndirectOffsetOnAxis(ap=st_idx[half][:, b:b + 1], axis=0),
                                    ).then_inc(got[b].sem, 16)

        @block.tensor
        def _(pe):
            def arrived(l, n, s):
                pe.wait_ge(w_in[s].sem, w_in[s].at(l, (n + 1) * 16))

            def norm_transposes(l, first):
                with pe.Fori(first, first + TILES) as t:
                    pe.wait_ge(n_xs.sem, n_xs.at(l, t + 1))
                    pe.wait_ge(n_ht.sem, n_ht.at(l, t))
                    for k in range(KD):
                        last = pe.transpose(ps[:, 4 + k // 4, (k % 4) * P:(k % 4 + 1) * P], XS[:, k * P:(k + 1) * P], ident)
                    last.then_inc(n_tp.sem, 1)

            pe.sem_inc(w_used.sem, WS)
            pe.wait_ge(silu_c.sem, 1)
            with pe.Fori(0, DEPTH) as l:
                pe.wait_ge(layer_done.sem, layer_done.at(l, 0))
                pe.sem_inc(pe_go.sem, 1)
                with pe.Fori(0, N_MOD // WS) as q:
                    for s in range(WS):
                        arrived(l, q, s)
                        pe.wait_ge(mod_ev.sem, mod_ev.at(l, q * WS + s + 1 - WS))
                        for c in range(2):
                            for k in range(KD):
                                last = pe.matmul(ps[:, s, 2 * c:2 * c + 2], Wt[s][:, k * 256 + c * P:k * 256 + c * P + P],
                                                 cT[:, k, :], start=(k == 0), stop=(k == KD - 1))
                        last.then_inc(w_used.sem, 1)
                norm_transposes(l, 0)

                pe.wait_ge(n_ht.sem, n_ht.at(l, TILES))
                for j in range(CJ):
                    arrived(l, AT_CP // WS, j)
                    pe.wait_ge(cp_ev.sem, cp_ev.at(l, j + 1 - 2))
                    bk = (j % 2) * 4
                    for c in range(2):
                        for bank, lo, hi in ((0, P, TOK), (1, 0, P)):
                            for k in range(KD):
                                last = pe.matmul(ps[:, bk + 2 * c + bank, 0:hi - lo],
                                                 Wt[j][:, k * 256 + c * P:k * 256 + c * P + P], hT[:, k, lo:hi],
                                                 start=(k == 0), stop=(k == KD - 1))
                    last.then_inc(w_used.sem, 1)

                pe.wait_ge(cp_ev.sem, cp_ev.at(l, CJ))
                pe.sem_inc(pe_go.sem, 1)
                with pe.Fori(0, N_QP // WS) as q:
                    for s in range(WS):
                        arrived(l, q + AT_QP // WS, s)
                        for t in range(TILES):
                            g = s * TILES + t
                            pe.wait_ge(qp_ev.sem, qp_ev.at(l, q * WS * TILES + g + 1 - 4))
                            for k in range(KD):
                                last = pe.matmul(ps[:, g % 4, 0:256], hT[:, k, t * P:(t + 1) * P],
                                                 Wt[s][:, k * 256:(k + 1) * 256], start=(k == 0), stop=(k == KD - 1))
                            last.then_inc(qp_ps.sem if t < TILES - 1 else w_used.sem, 1)

                pe.wait_ge(qp_ev.sem, qp_ev.at(l, N_QP * TILES))
                pe.wait_ge(tab_in.sem, tab_in.at(l, 16))
                for j in range(CJ):
                    pe.wait_ge(fo_g.sem, fo_g.at(l, j))
                    cols = slice(j * P, (j + 1) * P)
                    for c, tab in enumerate((C1, S1)):
                        for t in range(4):
                            pe.matmul(ps[:, 4 + 2 * c, :], Fin[:, t + 1, cols], CS[:, c, t, :], start=(t == 0), stop=(t == 3))
                        last = pe.matmul(ps[:, 5 + 2 * c, 0:P], Fin[:, 0, cols], tab, start=True, stop=True)
                    last.then_inc(fo_ps.sem, 1)
                    pe.wait_ge(fo_g.sem, fo_g.at(l, j + 1))
                    pe.wait_ge(fo_o.sem, fo_o.at(l, j))
                    for bank, lo, hi in ((0, P, TOK), (1, 0, P)):
                        pe.matmul(ps[:, bank, 0:hi - lo], BC, G[:, 0, lo:hi], start=True, stop=False)
                        last = pe.matmul(ps[:, bank, 0:hi - lo], BSn, G[:, 1, lo:hi], start=False, stop=True)
                    last.then_inc(fo_ops.sem, 1)

                pe.wait_ge(cv_y.sem, cv_y.at(l, 1))
                h = SPAN // 2
                for bank in range(2):
                    for j in range(CJ):
                        last = pe.matmul(ps[:, 2 + bank, 0:h], onesD, YC[:, j, bank * h:(bank + 1) * h],
                                         start=(j == 0), stop=(j == CJ - 1))
                last.then_inc(ln_mp.sem, 1)
                pe.wait_ge(ln_sq.sem, ln_sq.at(l, 1))
                for bank in range(2):
                    for j in range(CJ):
                        last = pe.matmul(ps[:, 6 + bank, 0:h], onesD, SQ[:, j, bank * h:(bank + 1) * h],
                                         start=(j == 0), stop=(j == CJ - 1))
                last.then_inc(ln_vp.sem, 1)

                pe.wait_ge(fo_o.sem, fo_o.at(l, CJ))
                pe.wait_ge(kq_ok.sem, kq_ok.at(l, 1))
                pe.sem_inc(pe_go.sem, 1)
                for t in range(TILES):
                    for i, c in enumerate((512, 576, 1152, 1216)):
                        last = pe.transpose(ps[0:HD, t, i * P:(i + 1) * P], TM[:, t, c:c + HD], ident)
                last.then_inc(kt_ps.sem, 1)
                pe.wait_ge(kt_ev.sem, kt_ev.at(l, 1))
                pe.wait_ge(kv_in.sem, kv_in.at(l, 64))
                pe.wait_ge(pads.sem, pads.at(l, 2))

                def attention(n, t):
                    u0 = n * UNITS
                    pe.wait_ge(qs_ok.sem, qs_ok.at(l, n + 1))
                    pe.wait_ge(a_exp.sem, a_exp.at(l, u0))
                    pe.sem_inc(pe_go.sem, 1)
                    for u in range(UNITS):
                        last = pe.transpose(ps[0:HD, u // 4, (u % 4) * P:(u % 4 + 1) * P], QO[:, u * HD:(u + 1) * HD], ident)
                    last.then_inc(qt_ps.sem, 1)
                    pe.wait_ge(qt_a.sem, qt_a.at(l, n + 1))
                    pe.wait_ge(qt_d.sem, qt_d.at(l, n + 1))

                    def scores(u):
                        pe.wait_ge(a_exp.sem, a_exp.at(l, u0 + u - 1))
                        pe.sem_inc(pe_go.sem, 1)
                        q, bk, kv = qT[:, u, :], (u % 2) * 2, (u % HEADS) // GROUP
                        if t is None:
                            keys = kTa[:, kv, 5 * P:6 * P] if u < HEADS else kTw[:, kv, 0:P]
                            last = pe.matmul(ps[:, bk, 0:P], q, keys, start=True, stop=True)
                        elif u < HEADS:
                            for i in range(2):
                                last = pe.matmul(ps[:, bk + i, 0:HALF], q, kTa[:, kv, i * HALF:(i + 1) * HALF],
                                                 start=True, stop=True)
                        else:
                            pe.matmul(ps[:, bk, 0:3 * P], q, kTw[:, kv, bass.ds(t * P, 3 * P)], start=True, stop=False)
                            pe.matmul(ps[:, bk, 0:P], ident, MK[:, bass.ds(t * 2 * P, P)], start=False, stop=False)
                            pe.matmul(ps[:, bk, 2 * P:3 * P], ident, MK[:, bass.ds(t * 2 * P + P, P)], start=False, stop=True)
                            last = pe.matmul(ps[:, bk, 3 * P:4 * P], q, kTw[:, kv, 6 * P:7 * P], start=True, stop=True)
                        last.then_inc(a_s.sem, 1)

                    def transposes(u):
                        pe.wait_ge(a_exp.sem, a_exp.at(l, u0 + u + 1))
                        pe.wait_ge(a_pa.sem, a_pa.at(l, u0 + u))
                        pe.wait_ge(a_pd.sem, a_pd.at(l, u0 + u))
                        if u < 2:
                            pe.wait_ge(ot_ev.sem, ot_ev.at(l, n))
                        split = dve_blocks(t, u)
                        for i in range(blocks(t, u)):
                            bank, o = (4, i) if i < split else (5, i - split)
                            last = pe.transpose(ps[:, bank, o * P:(o + 1) * P], Pb[u % 2][:, i * P:(i + 1) * P], ident)
                        last.then_inc(a_t.sem, 1)

                    def values(u):
                        pe.wait_ge(a_pa.sem, a_pa.at(l, u0 + u + 1))
                        pe.wait_ge(a_pd.sem, a_pd.at(l, u0 + u + 1))
                        pe.wait_ge(a_on.sem, a_on.at(l, u0 + u - 1))
                        kv = (u % HEADS) // GROUP
                        c = kv * HD + (u // HEADS) * P
                        if t is None:
                            vs = [V[:, 0, c:c + HD]]
                        elif u < HEADS:
                            vs = [V[:, b, c:c + HD] for b in (1, 2, 3, 4, 6)]
                        else:
                            flat = A[:, 2560:4352]
                            vs = [flat[:, bass.ds((t + i) * 256 + c, HD)] for i in range(3)] + [V[:, 6, c:c + HD]]
                        for i, v in enumerate(vs):
                            last = pe.matmul(ps[:, 6 + u % 2, 0:HD], PT[u % 2][:, i * P:(i + 1) * P], v,
                                             start=(i == 0), stop=(i == len(vs) - 1))
                        last.then_inc(a_o.sem, 1)

                    for u in range(UNITS + 2):
                        if u < UNITS:
                            scores(u)
                        if 1 <= u <= UNITS:
                            transposes(u - 1)
                        if u >= 2:
                            values(u - 2)
                    pe.wait_ge(a_on.sem, a_on.at(l, u0 + UNITS))
                    for i in range(8):
                        last = pe.transpose(ps[:, 4 + i // 4, (i % 4) * P:(i % 4 + 1) * P], QO[:, i * P:(i + 1) * P], ident)
                    last.then_inc(ot_ps.sem, 1)

                attention(0, None)
                with pe.Fori(0, TILES - 1) as t:
                    attention(t + 1, t)

                for i in range(8):
                    pe.wait_ge(rw_dg.sem, rw_dg.at(l, i + 1))
                    pe.wait_ge(rw_ev.sem, rw_ev.at(l, i - 1))
                    pe.matmul(ps[:, i % 2, :], onesD, T[:, 0:512], start=True, stop=True).then_inc(rw_ps.sem, 1)

                pe.wait_ge(rw_ev.sem, rw_ev.at(l, 8))
                pe.wait_ge(ot_ev.sem, ot_ev.at(l, TILES))
                pe.wait_ge(ln_o.sem, ln_o.at(l, 1))
                pe.sem_inc(pe_go.sem, 1)
                with pe.Fori(0, KD) as j:
                    for b in range(4):
                        arrived(l, j + AT_MG // WS, b)
                        bk = (b % 2) * 4
                        pe.wait_ge(mg_ev.sem, mg_ev.at(l, j * 4 + b - 1))
                        for i in range(2):
                            for k in range(KD):
                                last = pe.matmul(ps[:, bk + i, 0:HALF], Wt[b][:, k * P:(k + 1) * P],
                                                 hT[:, k, i * HALF:(i + 1) * HALF], start=(k == 0), stop=(k == KD - 1))
                        last.then_inc(mg_g.sem, 1)
                        for i in range(2):
                            for k in range(CJ):
                                last = pe.matmul(ps[:, bk + 2 + i, 0:HALF], Wt[b][:, (KD + k) * P:(KD + k + 1) * P],
                                                 BR[:, b, k, i * HALF:(i + 1) * HALF], start=(k == 0), stop=(k == CJ - 1))
                        last.then_inc(w_used.sem, 1)

                pe.wait_ge(mg_m.sem, mg_m.at(l, KD))
                for s in range(WS):
                    arrived(l, AT_OP // WS, s)
                for t in range(TILES):
                    bk = (t % 4) * 2
                    if t >= 4:
                        pe.wait_ge(op_x.sem, op_x.at(l, t - 3))
                    for c in range(4):
                        for k in range(KD):
                            last = pe.matmul(ps[:, bk + c // 2, (c % 2) * 256:(c % 2 + 1) * 256], mT[:, k, t * P:(t + 1) * P],
                                             Wt[c][:, k * 256:(k + 1) * 256], start=(k == 0), stop=(k == KD - 1))
                        if t == TILES - 1:
                            last.then_inc(w_used.sem, 1)
                    if t < TILES - 1:
                        last.then_inc(op_ps.sem, 1)

                norm_transposes(l, TILES)
                pe.wait_ge(n_ht.sem, n_ht.at(l, 2 * TILES))
                for t in range(TILES):
                    bk = (t % 2) * 2
                    if t >= 2:
                        pe.wait_ge(h2_ev.sem, h2_ev.at(l, t - 1))
                    for k in range(KD):
                        last = pe.transpose(ps[:, bk + k // 4, (k % 4) * P:(k % 4 + 1) * P], hT[:, k, t * P:(t + 1) * P], ident)
                    last.then_inc(h2_ps.sem, 1)

                pe.wait_ge(h2_ev.sem, h2_ev.at(l, TILES))
                pe.wait_ge(sk_in.sem, sk_in.at(l, 16))
                pe.sem_inc(pe_go.sem, 1)
                with pe.Fori(0, N_PQ // WS) as q:
                    def key_scores(i):
                        hp = q * 8 + i
                        pe.wait_ge(pq_q.sem, pq_q.at(l, hp + 1))
                        pe.wait_ge(pq_s.sem, pq_s.at(l, hp - 1))
                        for t in range(TILES):
                            last = pe.matmul(ps[:, (i % 2) * 2 + t // 4, (t % 4) * P:(t % 4 + 1) * P],
                                             QS[i % 2][:, t * P:(t + 1) * P], skT[:, i % 2, :], start=True, stop=True)
                        last.then_inc(pq_sp.sem, 1)

                    for i in range(8):
                        s = i // 2
                        if i % 2 == 0:
                            arrived(l, q + AT_PQ // WS, s)
                        for b in range(2):
                            for k in range(KD):
                                c = k * 256 + (i % 2) * P
                                last = pe.matmul(ps[:, 4 + (i % 2) * 2 + b, 0:HALF], Wt[s][:, c:c + P],
                                                 hT[:, k, b * HALF:(b + 1) * HALF], start=(k == 0), stop=(k == KD - 1))
                        last.then_inc(w_used.sem if i % 2 else pq_ps.sem, 1)
                        if i:
                            key_scores(i - 1)
                    key_scores(7)

        @block.scalar
        def _(act):
            def norm(l, first, kind):
                with act.Fori(0, TILES) as t:
                    act.wait_ge(n_ssq.sem, n_ssq.at(l, t + (first + 1)))
                    act.activation(s1[:, 1:2], s1[:, 0:1], ACT.Sqrt).then_inc(n_sq.sem, 1)
                    act.wait_ge(n_tp.sem, n_tp.at(l, t + (first + 1)))
                    af = aff[:, :, :, :].rearrange("p t c k -> p (t c k)")
                    for k in range(KD):
                        o = t * (4 * KD) + (2 * kind * KD + k)
                        last = act.activation(hT[:, k, bass.ds(t * P, P)], ps[:, 4 + k // 4, (k % 4) * P:(k % 4 + 1) * P],
                                              ACT.Identity, bias=af[:, bass.ds(o + KD, 1)], scale=af[:, bass.ds(o, 1)])
                    last.then_inc(n_ht.sem, 1)

            act.sem_inc(n_ht.sem, 1)
            act.sem_inc(qp_ev.sem, 4)
            act.sem_inc(fo_g.sem, 1)
            act.sem_inc(fo_o.sem, 1)
            act.sem_inc(a_exp.sem, 2)
            act.sem_inc(a_pa.sem, 1)
            act.sem_inc(ot_ev.sem, 1)
            act.sem_inc(rw_ev.sem, 2)
            act.wait_ge(cst_in.sem, 7 * 16)
            act.activation(cT[:, :, :], cT[:, :, :], ACT.Silu).then_inc(silu_c.sem, 1)
            with act.Fori(0, DEPTH) as l:
                ppl = pp[:, :, :].rearrange("p l n -> p (l n)")

                def par(name, i):
                    return ppl[:, bass.ds(l * PPW + (PP[name][0] + i), 1)]

                act.wait_ge(aff_ok.sem, aff_ok.at(l, 1))
                norm(l, 0, 0)
                for j in range(CJ):
                    act.wait_ge(w_used.sem, w_used.at(l, AT_CP + j + 1))
                    act.wait_ge(cp_ev.sem, cp_ev.at(l, j - 1))
                    bk = (j % 2) * 4 + 2
                    act.activation(G[:, j % 2, P:TOK], ps[:, bk, :], ACT.Sigmoid)
                    act.activation(G[:, j % 2, 0:P], ps[:, bk + 1, 0:P], ACT.Sigmoid).then_inc(cp_sg.sem, 1)
                act.wait_ge(pads.sem, pads.at(l, 1))
                for c in range(N_QP):
                    for t in range(TILES):
                        g = c * TILES + t
                        if t < TILES - 1:
                            act.wait_ge(qp_ps.sem, qp_ps.at(l, c * (TILES - 1) + t + 1))
                        else:
                            act.wait_ge(w_used.sem, w_used.at(l, AT_QP + c + 1))
                        src = ps[:, g % 4, 0:256]
                        if c < 2:
                            last = act.copy(Fin[:, t, c * 256:(c + 1) * 256], src)
                        elif c < 6:
                            o = (0, 256, 640, 896)[c - 2]
                            last = act.copy(TM[:, t, o:o + 256], src)
                        elif c == 6:
                            act.copy(TM[:, t, 512:640], src[:, 0:P])
                            last = act.copy(TM[:, t, 1152:1280], src[:, P:2 * P])
                        else:
                            last = act.copy(V[:, t, :], src)
                        last.then_inc(qp_ev.sem, 1)
                act.wait_ge(cp_ev.sem, cp_ev.at(l, CJ))
                for j in range(CJ):
                    act.wait_ge(fo_ps.sem, fo_ps.at(l, j + 1))
                    if j:
                        act.wait_ge(fo_ops.sem, fo_ops.at(l, j))
                    for c in range(2):
                        act.copy(G[:, c, P:TOK], ps[:, 4 + 2 * c, :])
                        last = act.copy(G[:, c, 0:P], ps[:, 5 + 2 * c, 0:P])
                    last.then_inc(fo_g.sem, 1)
                    act.wait_ge(fo_ops.sem, fo_ops.at(l, j + 1))
                    act.copy(BR[:, 0, j, P:TOK], ps[:, 0, :])
                    act.copy(BR[:, 0, j, 0:P], ps[:, 1, 0:P]).then_inc(fo_o.sem, 1)
                act.wait_ge(ln_d.sem, ln_d.at(l, 1))
                act.activation(SQ, YC, ACT.Square).then_inc(ln_sq.sem, 1)
                act.wait_ge(ln_v.sem, ln_v.at(l, 1))
                act.activation(RSTD, RSTD, ACT.Sqrt).then_inc(ln_sr.sem, 1)
                act.wait_ge(ln_n.sem, ln_n.at(l, 1))
                for j in range(CJ):
                    act.activation(BR[:, 1, j, 0:P], YC[:, j, 0:P], ACT.Silu, bias=par("lb", j), scale=par("lg", j))
                    last = act.activation(BR[:, 1, j, P:TOK], YC[:, j, P + 2 * PAD:SPAN], ACT.Silu,
                                          bias=par("lb", j), scale=par("lg", j))
                last.then_inc(ln_o.sem, 1)
                with act.Fori(0, TILES) as t:
                    act.wait_ge(kq_s.sem, kq_s.at(l, t + 1))
                    act.activation(nrm[:, 1, :], nrm[:, 0, :], ACT.Sqrt).then_inc(kq_r.sem, 1)
                act.wait_ge(kt_ps.sem, kt_ps.at(l, 1))
                for t in range(TILES):
                    blk = 5 if t == 0 else t - 1
                    act.copy(kTa[:, :, blk * P:(blk + 1) * P], ps[0:HD, t, 0:256].rearrange("p (v n) -> p v n", v=2))
                    last = act.copy(kTw[:, :, t * P:(t + 1) * P], ps[0:HD, t, 256:512].rearrange("p (v n) -> p v n", v=2))
                last.then_inc(kt_ev.sem, 1)

                def attention(n, t):
                    u0 = n * UNITS
                    if t is not None:
                        act.wait_ge(ot_ps.sem, ot_ps.at(l, n))
                    flat = A[:, 4352:10752]
                    base = n * 1280
                    act.copy(QO[:, 0:512], flat[:, bass.ds(base, 512)])
                    act.copy(QO[:, 512:1024], flat[:, bass.ds(base + 640, 512)]).then_inc(qs_ok.sem, 1)
                    act.wait_ge(qt_ps.sem, qt_ps.at(l, n + 1))
                    act.copy(qT[:, 0:8, :], ps[0:HD, 0:2, :].rearrange("p b (u n) -> p (b u) n", n=P)).then_inc(qt_a.sem, 1)

                    def exps(u):
                        act.wait_ge(a_m.sem, a_m.at(l, u0 + u + 1))
                        if u >= 2:
                            act.wait_ge(a_t.sem, a_t.at(l, u0 + u - 1))
                        bk, e = (u % 2) * 2, u % 2
                        nb = blocks(t, u)
                        if nb == 5:
                            src = ps[:, bk:bk + 2, 0:HALF]
                            dst = Pb[e].rearrange("p (i n) -> p i n", i=2)
                        else:
                            src, dst = ps[:, bk, 0:nb * P], Pb[e][:, 0:nb * P]
                        if u >= HEADS:
                            h = u - HEADS
                            act.activation(sm[:, 3, e:e + 1], nsink[:, h:h + 1], ACT.Exp, bias=sm[:, 1, e:e + 1], scale=-1.0)
                        act.activation(dst, src, ACT.Exp, bias=sm[:, 1, e:e + 1], scale=SCALE,
                                       accum_out=sm[:, 2, e:e + 1]).then_inc(a_exp.sem, 1)

                    def pt_copy(u):
                        nb, split = blocks(t, u), dve_blocks(t, u)
                        if nb == split:
                            act.sem_inc(a_pa.sem, 1)
                            return
                        act.wait_ge(a_t.sem, a_t.at(l, u0 + u + 1))
                        if u >= 2:
                            act.wait_ge(a_o.sem, a_o.at(l, u0 + u - 1))
                        act.copy(PT[u % 2][:, split * P:nb * P], ps[:, 5, 0:(nb - split) * P]).then_inc(a_pa.sem, 1)

                    for u in range(UNITS + 1):
                        if u < UNITS:
                            exps(u)
                        if u:
                            pt_copy(u - 1)
                    act.wait_ge(ot_ps.sem, ot_ps.at(l, n + 1))
                    brf = B[:, 5120:10240].rearrange("p (b n) -> p b n", b=8)
                    act.copy(brf[:, :, bass.ds(n * P, P)],
                             ps[:, 4:6, :].rearrange("p b (j n) -> p (b j) n", n=P)).then_inc(ot_ev.sem, 1)

                attention(0, None)
                with act.Fori(0, TILES - 1) as t:
                    attention(t + 1, t)

                for i in range(8):
                    act.wait_ge(rw_ps.sem, rw_ps.at(l, i + 1))
                    act.activation(grow[:, i // 4, (i // 2) % 2, (i % 2) * 512:(i % 2 + 1) * 512], ps[:, i % 2, :],
                                   ACT.Copy, scale=float(CONV)).then_inc(rw_ev.sem, 1)
                with act.Fori(0, KD) as j:
                    for b in range(4):
                        act.wait_ge(mg_g.sem, mg_g.at(l, j * 4 + b + 1))
                        act.wait_ge(mg_ev.sem, mg_ev.at(l, j * 4 + b - 1))
                        act.activation(SG[b % 2].rearrange("p (i n) -> p i n", i=2), ps[:, (b % 2) * 4:(b % 2) * 4 + 2, 0:HALF],
                                       ACT.Sigmoid, bias=ppl[:, bass.ds(l * PPW + j + (PP["bg"][0] + b * KD), 1)])\
                            .then_inc(mg_sg.sem, 1)
                norm(l, TILES, 1)
                for t in range(TILES):
                    act.wait_ge(h2_ps.sem, h2_ps.at(l, t + 1))
                    act.copy(h2[:, t, :].rearrange("p (b n) -> p b n", b=2), ps[:, (t % 2) * 2:(t % 2) * 2 + 2, :])\
                        .then_inc(h2_ev.sem, 1)
                with act.Fori(0, UNITS // 2) as q:
                    for i in range(2):
                        if i == 0:
                            act.wait_ge(pq_ps.sem, pq_ps.at(l, q + 1))
                        else:
                            act.wait_ge(w_used.sem, w_used.at(l, q + (AT_PQ + 1)))
                        act.wait_ge(pq_s.sem, pq_s.at(l, q * 2 + i - 1))
                        act.copy(QS[i].rearrange("p (b n) -> p b n", b=2), ps[:, 4 + 2 * i:6 + 2 * i, 0:HALF])\
                            .then_inc(pq_q.sem, 1)

                def gate_exp(t):
                    act.wait_ge(tk_d.sem, tk_d.at(l, t + 1))
                    act.activation(topw[:, 0, :], topw[:, 0, :], ACT.Exp).then_inc(tk_e.sem, 1)

                def stage(t, uv):
                    with act.Fori(0, GROUPS // 2) as q:
                        for half in range(2):
                            m = (t * 2 + uv) * GROUPS + q * 2 + half
                            act.wait_ge(used.sem, used.at(l, (m - 1) * RING))
                            act.copy(st_idx[half][:, :], EI[:, bass.ds(t * SLOTS + (q * 2 + half) * RING, RING)])\
                                .then_inc(st_ok.sem, 1)

                gate_exp(0)
                act.wait_ge(ei_ok.sem, ei_ok.at(l, 1))

                def tile(t, more):
                    stage(t, 0)
                    act.wait_ge(u_done.sem, u_done.at(l, t + 1))
                    act.activation(dots[:, :], dots[:, :], ACT.Gelu_apprx_tanh).then_inc(u_act.sem, 1)
                    if more:
                        gate_exp(t + 1)
                        act.wait_ge(ei_ok.sem, ei_ok.at(l, t + 2))
                    stage(t, 1)

                with act.Fori(0, TILES - 1) as t:
                    tile(t, True)
                tile(TILES - 1, False)
            for t in range(TILES):
                act.wait_ge(f_ss.sem, t + 1)
                act.activation(s1[:, 1:2], s1[:, 0:1], ACT.Sqrt).then_inc(f_sq.sem, 1)

        @block.vector
        def _(v):
            def mean_square(src):
                v.scalar_tensor_tensor(out=JX, in0=src, scalar=1.0, in1=src, op0=ALU.mult, op1=ALU.mult,
                                       accum_out=s1[:, 2:3])
                v.drain()
                return v.tensor_scalar(out=s1[:, 0:1], in0=s1[:, 2:3], scalar1=1.0 / D, scalar2=EPS, op0=ALU.mult, op1=ALU.add)

            def norm(l, first):
                with v.Fori(0, TILES) as t:
                    src = xf[:, bass.ds(t * D, D)]
                    v.drain()
                    mean_square(src).then_inc(n_ssq.sem, 1)
                    v.wait_ge(n_sq.sem, n_sq.at(l, t + (first + 1)))
                    v.reciprocal(s1[:, 3:4], s1[:, 1:2])
                    v.drain()
                    v.wait_ge(n_ht.sem, n_ht.at(l, t + first))
                    v.tensor_scalar(out=XS, in0=src, scalar1=s1[:, 3:4], scalar2=None, op0=ALU.mult).then_inc(n_xs.sem, 1)

            xf = x[:, :, :].rearrange("p t n -> p (t n)")
            v.sem_inc(mod_ev.sem, WS)
            v.sem_inc(cp_ev.sem, 2)
            v.sem_inc(a_pd.sem, 1)
            v.sem_inc(a_on.sem, 2)
            v.sem_inc(mg_ev.sem, 2)
            v.sem_inc(pq_s.sem, 2)
            v.sem_inc(used.sem, RING)
            v.wait_ge(cst_in.sem, 7 * 16)
            v.sem_inc(layer_done.sem, 1)
            with v.Fori(0, DEPTH) as l:
                ppl = pp[:, :, :].rearrange("p l n -> p (l n)")
                rowl = row[:, :, :].rearrange("p l n -> p (l n)")

                def par(name, i=0, n=1):
                    return ppl[:, bass.ds(l * PPW + (PP[name][0] + i), n)]

                def rowp(o, n):
                    return rowl[:, bass.ds(l * (2 * HD + HEADS) + o, n)]

                adf = adaT[:, :, :].rearrange("p j s -> p (j s)")
                with v.Fori(0, N_MOD // WS) as q:
                    for s in range(WS):
                        n = q * WS + s
                        v.wait_ge(w_used.sem, w_used.at(l, n + 1))
                        b = ppl[:, bass.ds(l * PPW + n * 2 + PP["bada"][0], 2)]
                        v.tensor_tensor(out=adf[:, bass.ds(n * 4, 4)].rearrange("p (j s) -> p j s", j=2),
                                        in0=ps[:, s, 0:4].rearrange("p (j s) -> p j s", j=2),
                                        in1=b.unsqueeze(2).broadcast_to([P, 2, 2]), op=ALU.add).then_inc(mod_ev.sem, 1)
                v.drain()
                for kind in range(2):
                    gain = par(("n1", "n2")[kind], 0, KD)
                    for s, t0, nt in ((0, 0, 1), (1, 1, 4)):
                        sc = adaT[:, (1 + 3 * kind) * KD:(2 + 3 * kind) * KD, s]
                        sh = adaT[:, 3 * kind * KD:(3 * kind + 1) * KD, s]
                        for t in range(t0, t0 + nt):
                            v.scalar_tensor_tensor(out=aff[:, t, 2 * kind, :], in0=sc, scalar=1.0, in1=gain,
                                                   op0=ALU.add, op1=ALU.mult)
                            v.tensor_copy(aff[:, t, 2 * kind + 1, :], sh)
                v.tensor_scalar(out=nsink[:, :], in0=rowp(2 * HD, HEADS), scalar1=-1.0, scalar2=None, op0=ALU.mult)\
                    .then_inc(aff_ok.sem, 1)
                norm(l, 0)
                v.wait_ge(pads.sem, pads.at(l, 1))
                for j in range(CJ):
                    v.wait_ge(cp_sg.sem, cp_sg.at(l, j + 1))
                    bk = (j % 2) * 4
                    v.tensor_tensor(out=convh[:, j, PAD:PAD + P], in0=ps[:, bk + 1, 0:P], in1=G[:, j % 2, 0:P], op=ALU.mult)
                    v.tensor_tensor(out=convh[:, j, 3 * PAD + P:3 * PAD + TOK], in0=ps[:, bk, :], in1=G[:, j % 2, P:TOK],
                                    op=ALU.mult).then_inc(cp_ev.sem, 1)
                v.drain()
                for j in range(CJ):
                    v.tensor_scalar(out=YC[:, j, :], in0=convh[:, j, 0:SPAN], scalar1=par("cw", j * TAPS),
                                    scalar2=par("cb", j), op0=ALU.mult, op1=ALU.add)
                chf = M[:, 0:CJ * CPAD]
                with v.Fori(1, TAPS) as k:
                    v.drain()
                    for j in range(CJ):
                        v.scalar_tensor_tensor(out=YC[:, j, :], in0=chf[:, bass.ds(k + j * CPAD, SPAN)],
                                               scalar=ppl[:, bass.ds(l * PPW + k + (PP["cw"][0] + j * TAPS), 1)],
                                               in1=YC[:, j, :], op0=ALU.mult, op1=ALU.add)
                v.drain().then_inc(cv_y.sem, 1)
                h = SPAN // 2
                v.wait_ge(ln_mp.sem, ln_mp.at(l, 1))
                for j in range(CJ):
                    y2 = YC[:, j, :].rearrange("p (b n) -> p b n", b=2)
                    last = v.tensor_tensor(out=y2, in0=y2, in1=ps[:, 2:4, 0:h], op=ALU.subtract)
                last.then_inc(ln_d.sem, 1)
                v.wait_ge(ln_vp.sem, ln_vp.at(l, 1))
                v.tensor_scalar(out=RSTD.rearrange("p (b n) -> p b n", b=2), in0=ps[:, 6:8, 0:h], scalar1=EPS, scalar2=None,
                                op0=ALU.add).then_inc(ln_v.sem, 1)
                v.wait_ge(ln_sr.sem, ln_sr.at(l, 1))
                v.reciprocal(RSTD, RSTD)
                v.drain()
                for j in range(CJ):
                    last = v.tensor_tensor(out=YC[:, j, :], in0=YC[:, j, :], in1=RSTD, op=ALU.mult)
                last.then_inc(ln_n.sem, 1)

                v.wait_ge(qp_ev.sem, qp_ev.at(l, N_QP * TILES))
                v.sem_inc(dve_go.sem, 1)
                tmf = A[:, 4352:10752]
                with v.Fori(0, TILES) as t:
                    heads = tmf[:, bass.ds(t * 1280, 640)].rearrange("p (h d) -> p h d", d=HD)
                    sq = T[:, :].rearrange("p (h d) -> p h d", d=HD)
                    v.drain()
                    v.tensor_tensor(out=sq, in0=heads, in1=heads, op=ALU.mult)
                    v.drain()
                    v.tensor_reduce(out=nrm[:, 2, :], in_=sq, axis=AX.X, op=ALU.add)
                    v.drain()
                    v.tensor_scalar(out=nrm[:, 0, :], in0=nrm[:, 2, :], scalar1=1.0 / HD, scalar2=EPS, op0=ALU.mult,
                                    op1=ALU.add).then_inc(kq_s.sem, 1)
                    v.wait_ge(kq_r.sem, kq_r.at(l, t + 1))
                    v.reciprocal(nrm[:, 2, :], nrm[:, 1, :])
                    v.drain()
                    v.tensor_tensor(out=heads, in0=heads, in1=nrm[:, 2, :].unsqueeze(2).broadcast_to([P, 10, HD]), op=ALU.mult)
                    v.drain()
                    for o, lo, hi in ((0, 0, HEADS), (HD, HEADS, HEADS + KVH)):
                        hh = tmf[:, bass.ds(t * 1280 + lo * HD, (hi - lo) * HD)].rearrange("p (h d) -> p h d", d=HD)
                        v.tensor_tensor(out=hh, in0=hh, in1=rowp(o, HD).unsqueeze(1).broadcast_to([P, hi - lo, HD]), op=ALU.mult)
                rpf = rope[:, :, :, :].rearrange("p c t d -> p (c t d)")
                with v.Fori(0, TILES - 1) as t:
                    for part in range(2):
                        heads = tmf[:, bass.ds(t * 1280 + (1280 + part * 640), 640)].rearrange("p (h d) -> p h d", d=HD)
                        sw = T[:, :].rearrange("p (h d) -> p h d", d=HD)
                        hd = HD // 2
                        v.drain()
                        for a, b in ((0, hd), (hd, 0)):
                            v.tensor_tensor(out=sw[:, :, a:a + hd], in0=heads[:, :, b:b + hd],
                                            in1=rpf[:, bass.ds(t * HD + (4 * HD + a), hd)].unsqueeze(1).broadcast_to([P, 10, hd]),
                                            op=ALU.mult)
                        v.drain()
                        v.tensor_tensor(out=heads, in0=heads,
                                        in1=rpf[:, bass.ds(t * HD, HD)].unsqueeze(1).broadcast_to([P, 10, HD]), op=ALU.mult)
                        v.drain()
                        v.tensor_tensor(out=heads, in0=heads, in1=sw, op=ALU.add)
                v.drain().then_inc(kq_ok.sem, 1)

                def attention(n, t):
                    u0 = n * UNITS
                    v.wait_ge(qt_ps.sem, qt_ps.at(l, n + 1))
                    v.tensor_copy(qT[:, 8:16, :], ps[0:HD, 2:4, :].rearrange("p b (u n) -> p (b u) n", n=P)).then_inc(qt_d.sem, 1)

                    def maxima(u):
                        bk, e = (u % 2) * 2, u % 2
                        nb = blocks(t, u)
                        v.wait_ge(a_s.sem, a_s.at(l, u0 + u + 1))
                        if nb == 5:
                            v.tensor_reduce(out=sm[:, 0, e:e + 1], in_=ps[:, bk:bk + 2, 0:HALF], axis=AX.XY, op=ALU.max)
                        else:
                            v.tensor_reduce(out=sm[:, 0, e:e + 1], in_=ps[:, bk, 0:nb * P], axis=AX.X, op=ALU.max)
                        v.drain()
                        if u < HEADS:
                            last = v.tensor_scalar(out=sm[:, 1, e:e + 1], in0=sm[:, 0, e:e + 1], scalar1=-SCALE, scalar2=None,
                                                   op0=ALU.mult)
                        else:
                            last = v.tensor_scalar(out=sm[:, 1, e:e + 1], in0=sm[:, 0, e:e + 1], scalar1=-SCALE,
                                                   scalar2=nsink[:, u - HEADS:u - HEADS + 1], op0=ALU.mult, op1=ALU.min)
                        last.then_inc(a_m.sem, 1)

                    def pt_copy(u):
                        w = dve_blocks(t, u) * P
                        e = u % 2
                        v.wait_ge(a_t.sem, a_t.at(l, u0 + u + 1))
                        if u >= 2:
                            v.wait_ge(a_o.sem, a_o.at(l, u0 + u - 1))
                        v.tensor_copy(PT[e][:, 0:w], ps[:, 4, 0:w]).then_inc(a_pd.sem, 1)
                        if u >= HEADS:
                            v.tensor_tensor(out=sm[:, 5, e:e + 1], in0=sm[:, 2, e:e + 1], in1=sm[:, 3, e:e + 1], op=ALU.add)
                            v.drain()
                            v.reciprocal(sm[:, 4, e:e + 1], sm[:, 5, e:e + 1])
                        else:
                            v.reciprocal(sm[:, 4, e:e + 1], sm[:, 2, e:e + 1])
                        v.drain()

                    def out(u):
                        v.wait_ge(a_o.sem, a_o.at(l, u0 + u + 1))
                        v.tensor_scalar(out=QO[:, u * HD:(u + 1) * HD], in0=ps[:, 6 + u % 2, 0:HD],
                                        scalar1=sm[:, 4, u % 2:u % 2 + 1], scalar2=None, op0=ALU.mult).then_inc(a_on.sem, 1)

                    for u in range(UNITS + 2):
                        if u >= 2:
                            out(u - 2)
                        if u < UNITS:
                            maxima(u)
                        if 1 <= u <= UNITS:
                            pt_copy(u - 1)

                attention(0, None)
                with v.Fori(0, TILES - 1) as t:
                    attention(t + 1, t)

                for i in range(8):
                    if i:
                        v.wait_ge(rw_ps.sem, rw_ps.at(l, i))
                    j0 = (2 + 3 * (i // 4)) * KD + (i % 2) * 4
                    v.tensor_tensor(out=T[:, 0:512].rearrange("p (j n) -> p j n", j=4),
                                    in0=ident.unsqueeze(1).broadcast_to([P, 4, P]),
                                    in1=adaT[:, j0:j0 + 4, (i // 2) % 2].unsqueeze(2).broadcast_to([P, 4, P]),
                                    op=ALU.mult).then_inc(rw_dg.sem, 1)
                mf = M[:, :]
                with v.Fori(0, KD) as j:
                    for b in range(4):
                        v.wait_ge(mg_sg.sem, mg_sg.at(l, j * 4 + b + 1))
                        v.wait_ge(w_used.sem, w_used.at(l, j * 4 + (b + AT_MG + 1)))
                        bk = (b % 2) * 4 + 2
                        dst = mf[:, bass.ds(j * TOK, TOK)]
                        to = dst if b == 0 else PR
                        v.tensor_tensor(out=to.rearrange("p (b n) -> p b n", b=2), in0=ps[:, bk:bk + 2, 0:HALF],
                                        in1=SG[b % 2].rearrange("p (b n) -> p b n", b=2), op=ALU.mult).then_inc(mg_ev.sem, 1)
                        v.drain()
                        if b:
                            v.tensor_tensor(out=dst, in0=dst, in1=PR, op=ALU.add)
                            last = v.drain()
                    last.then_inc(mg_m.sem, 1)
                for t in range(TILES):
                    bk = (t % 4) * 2
                    if t < TILES - 1:
                        v.wait_ge(op_ps.sem, op_ps.at(l, t + 1))
                    else:
                        v.wait_ge(w_used.sem, w_used.at(l, AT_PQ))
                    v.tensor_tensor(out=JX.rearrange("p (b n) -> p b n", b=2), in0=ps[:, bk:bk + 2, :],
                                    in1=grow[:, 0, min(t, 1), :].rearrange("p (b n) -> p b n", b=2), op=ALU.mult).then_inc(op_x.sem, 1)
                    v.drain()
                    v.tensor_tensor(out=x[:, t, :], in0=x[:, t, :], in1=JX, op=ALU.add)
                    v.drain()
                norm(l, TILES)
                v.wait_ge(nk_done.sem, nk_done.at(l, 64))
                v.sem_inc(dve_go.sem, 1)
                scf = A[:, 0:10240].rearrange("p (t n) -> p t n", t=TILES)
                with v.Fori(0, UNITS // 2) as q:
                    for i in range(2):
                        hp = q * 2 + i
                        v.wait_ge(pq_sp.sem, pq_sp.at(l, hp + 1))
                        v.tensor_copy(scf[:, 0:4, bass.ds(hp * P, P)], ps[:, 2 * i, :].rearrange("p (t n) -> p t n", n=P))
                        v.tensor_copy(scf[:, 4, bass.ds(hp * P, P)], ps[:, 2 * i + 1, 0:P]).then_inc(pq_s.sem, 1)
                v.drain()

                def top16(values, val, idx, n):
                    for r in range(n):
                        v.max(val(r, 0), values(r))
                    v.drain()
                    for r in range(n):
                        v.max_index(idx(r, 0), val(r, 0), values(r))
                    v.drain()
                    for r in range(n):
                        v.match_replace(values(r), val(r, 0), values(r), -3e38)
                    v.drain()
                    for r in range(n):
                        v.max(val(r, 1), values(r))
                    v.drain()
                    for r in range(n):
                        v.max_index(idx(r, 1), val(r, 1), values(r))
                    v.drain()

                def experts(t):
                    scores = B[:, RING * 1024:(RING + 2) * 1024]
                    v.tensor_copy(scores, A[:, bass.ds(t * (UNITS * P), UNITS * P)])
                    v.drain()
                    top16(lambda r: scores[:, r * P:(r + 1) * P],
                          lambda r, i: S16[:, r, i * 8:(i + 1) * 8], lambda r, i: I16[:, r, i * 8:(i + 1) * 8], UNITS)
                    v.tensor_copy(F16, I16)
                    s4 = S16.rearrange("p (h c) k -> p h c k", c=2)
                    for h in range(PH):
                        v.tensor_tensor(out=cand[:, h, :].rearrange("p (a b) -> p a b", a=TOPK),
                                        in0=s4[:, h, 0, :].unsqueeze(2).broadcast_to([P, TOPK, TOPK]),
                                        in1=s4[:, h, 1, :].unsqueeze(1).broadcast_to([P, TOPK, TOPK]), op=ALU.add)
                    v.drain()
                    top16(lambda r: cand[:, r, :], lambda r, i: TS[:, r, i * 8:(i + 1) * 8],
                          lambda r, i: TP[:, r, i * 8:(i + 1) * 8], PH)
                    w3 = [topw[:, i, :].rearrange("p (h k) -> p h k", h=PH) for i in range(4)]
                    v.tensor_tensor(out=w3[0], in0=TS, in1=TS[:, :, 0:1].broadcast_to([P, PH, TOPK]), op=ALU.subtract)\
                        .then_inc(tk_d.sem, 1)
                    v.tensor_scalar(out=w3[3].bitcast(U32), in0=TP, scalar1=TOPK * (TOPK - 1), scalar2=None,
                                    op0=ALU.bitwise_and)
                    v.tensor_scalar(out=w3[2].bitcast(U32), in0=TP, scalar1=TOPK - 1, scalar2=None, op0=ALU.bitwise_and)
                    v.drain()
                    v.tensor_copy(w3[1], w3[3].bitcast(U32))
                    v.tensor_copy(TS, w3[2].bitcast(U32))
                    v.drain()
                    f4 = F16.rearrange("p (h c) k -> p h c k", c=2)
                    for c, pos, res in ((0, w3[1], 3), (1, TS, 2)):
                        v.tensor_tensor(out=EQ, in0=pos.unsqueeze(3).broadcast_to([P, PH, TOPK, TOPK]),
                                        in1=io[:, c * TOPK:(c + 1) * TOPK].unsqueeze(1).unsqueeze(1).broadcast_to([P, PH, TOPK, TOPK]),
                                        op=ALU.is_equal)
                        v.drain()
                        v.tensor_tensor(out=EQ, in0=EQ, in1=f4[:, :, c, :].unsqueeze(2).broadcast_to([P, PH, TOPK, TOPK]),
                                        op=ALU.mult)
                        v.drain()
                        v.tensor_reduce(out=w3[res], in_=EQ, axis=AX.X, op=ALU.add)
                        v.drain()
                    v.scalar_tensor_tensor(out=w3[1], in0=w3[3], scalar=float(P), in1=w3[2], op0=ALU.mult, op1=ALU.add)
                    v.drain()
                    v.tensor_scalar(out=EI[:, bass.ds(t * SLOTS, SLOTS)], in0=topw[:, 1, :],
                                    scalar1=io[:, bass.ds(l + 2 * TOPK, 1)], scalar2=None, op0=ALU.add).then_inc(ei_ok.sem, 1)
                    v.wait_ge(tk_e.sem, tk_e.at(l, t + 1))
                    v.tensor_reduce(out=s1[:, 8:16], in_=w3[0], axis=AX.X, op=ALU.add)
                    v.drain()
                    v.reciprocal(s1[:, 0:8], s1[:, 8:16])
                    v.drain()
                    v.tensor_tensor(out=GT[:, bass.ds(t * SLOTS, SLOTS)].rearrange("p (h k) -> p h k", h=PH), in0=w3[0],
                                    in1=s1[:, 0:8].unsqueeze(2).broadcast_to([P, PH, TOPK]), op=ALU.mult)
                    v.drain()

                def products(t):
                    m0 = t * 2 * GROUPS
                    with v.Fori(0, GROUPS) as g:
                        for b in range(RING):
                            v.wait_ge(got[b].sem, got[b].at(l, (m0 + g + 1) * 16))
                            v.wait_ge(used.sem, used.at(l, (m0 + g) * RING + b - 1))
                            v.scalar_tensor_tensor(out=junk[b % 2], in0=ring[b], scalar=1.0, in1=M[:, bass.ds(t * D, D)],
                                                   op0=ALU.mult, op1=ALU.mult, accum_out=dots[:, bass.ds(g * RING + b, 1)])\
                                .then_inc(used.sem, 1)
                    v.drain().then_inc(u_done.sem, 1)

                def sums(t, s):
                    m0 = (t * 2 + 1) * GROUPS
                    v.wait_ge(u_act.sem, u_act.at(l, t + 1))
                    v.tensor_tensor(out=wgt[:, :], in0=dots[:, :], in1=GT[:, bass.ds(t * SLOTS, SLOTS)], op=ALU.mult)
                    for a in acc:
                        v.memset(a, 0.0)
                    v.drain()
                    with v.Fori(0, GROUPS) as g:
                        for b in range(RING):
                            v.wait_ge(got[b].sem, got[b].at(l, (m0 + g + 1) * 16))
                            v.wait_ge(used.sem, used.at(l, (m0 + g) * RING + b - 1))
                            v.scalar_tensor_tensor(out=acc[b % 2], in0=ring[b], scalar=wgt[:, bass.ds(g * RING + b, 1)],
                                                   in1=acc[b % 2], op0=ALU.mult, op1=ALU.add).then_inc(used.sem, 1)
                    v.drain()
                    v.tensor_tensor(out=acc[0], in0=acc[0], in1=acc[1], op=ALU.add)
                    v.drain()
                    v.tensor_tensor(out=acc[0], in0=acc[0], in1=grow[:, 1, s, :], op=ALU.mult)
                    v.drain()
                    xt = xf[:, bass.ds(t * D, D)]
                    v.tensor_tensor(out=xt, in0=xt, in1=acc[0], op=ALU.add)
                    v.drain()

                experts(0)
                products(0)
                experts(1)
                sums(0, 0)
                with v.Fori(1, TILES - 1) as t:
                    products(t)
                    experts(t + 1)
                    sums(t, 1)
                products(TILES - 1)
                sums(TILES - 1, 1)
                v.drain().then_inc(layer_done.sem, 1)

            v.wait_ge(f_g.sem, 16)
            for t in range(TILES):
                mean_square(x[:, t, :]).then_inc(f_ss.sem, 1)
                v.wait_ge(f_sq.sem, t + 1)
                v.reciprocal(s1[:, 3:4], s1[:, 1:2])
                v.drain()
                v.scalar_tensor_tensor(out=h2[:, t, :], in0=x[:, t, :], scalar=s1[:, 3:4], in1=R[:, 0:D],
                                       op0=ALU.mult, op1=ALU.mult).then_inc(f_y.sem, 1)
                v.drain()


def blocks(t, u):
    return 1 if t is None else 5 if u < HEADS else 4


def dve_blocks(t, u):
    return (blocks(t, u) + 1) // 2


def shape_constants():
    f8 = np.float64
    eye = np.eye(P, dtype=np.float32)
    ones = np.full((P, P), 1.0 / CONV, np.float32)

    def dft(n):
        a = 2 * np.pi * ((np.arange(n)[:, None] * np.arange(n)[None, :]) % n).astype(f8) / n
        return np.cos(a) / np.sqrt(n), np.sin(a) / np.sqrt(n)

    c64, s64 = dft(HD)
    z = np.zeros((HD, HD))
    bc, bs = np.block([[c64, z], [z, c64]]), -np.block([[s64, z], [z, s64]])
    c1, s1 = dft(P)
    nf = HD // 4
    inv = (1.0 / (np.float32(10000.0) ** (np.arange(nf, dtype=np.float32) / np.float32(nf)))).astype(np.float32)
    pos = np.arange(LAT)
    ang = np.concatenate([(pos // 64).astype(np.float32)[:, None] * inv, (pos % 64).astype(np.float32)[:, None] * inv], -1)
    c, s = np.cos(ang), np.sin(ang)
    cc, ss = np.concatenate([c, c], -1), np.concatenate([-s, s], -1)
    rope = np.stack([cc, ss]).reshape(2, 4, P, HD).transpose(2, 0, 1, 3).reshape(P, -1)
    io = np.concatenate([np.arange(TOPK) * TOPK, np.arange(TOPK), np.arange(DEPTH) * EXPERTS])
    io = np.broadcast_to(io, (P, io.size))
    cst = np.concatenate([eye, ones, bc, bs, rope, io], 1).astype(np.float32)
    tab = np.concatenate([m.reshape(4, P, LAT).transpose(1, 0, 2).reshape(P, -1) for m in dft(LAT)] + [c1, s1], 1)
    tab = tab.astype(np.float32)
    q, k = np.arange(P)[:, None], np.arange(P)[None, :]
    lo, up, no = np.where(k >= q, 0, NEG), np.where(k <= q, 0, NEG), np.full((P, P), NEG)
    mask = np.concatenate([m for t in range(4) for m in (no if t == 0 else lo, no if t == 3 else up)], 1).astype(np.float32)
    return cst, tab, mask


def kernel(**inp):
    import concourse.bacc as bacc
    from concourse.bass_utils import run_bass_kernel_spmd as run

    g = {k: np.asarray(v) for k, v in inp.items()}

    def cols(w, width=256):
        d, k, n = w.shape
        return w.reshape(d, k // P, P, n // width, width).transpose(0, 3, 2, 1, 4).reshape(d, n // width, P, -1)

    w_in = g["w_in"]
    f, c_a, c_g, aq, ak, av, wq, wk, wv, gl = np.split(
        w_in, np.cumsum([512, 512, 512, 512, 128, 128, 512, 128, 128]), axis=2)
    conv = np.stack([c_a.reshape(DEPTH, D, CJ, P), c_g.reshape(DEPTH, D, CJ, P)], 3).reshape(DEPTH, D, 1024)
    branch = [g["w_fourier_out"], g["w_conv_out"], g["w_attn_out"], g["w_win_out"]]
    merge = []
    for b in range(4):
        gates = cols(gl[:, :, b * D:(b + 1) * D], P)
        merge.append(np.concatenate([gates, cols(branch[b], P), np.zeros((DEPTH, KD, P, 512), np.float32)], 3))
    merge = np.stack(merge, 2).reshape(DEPTH, N_MG, P, SLOT_W)
    ws = np.concatenate([cols(g["w_ada"]), cols(conv), cols(f), cols(aq), cols(wq), cols(np.concatenate([ak, wk, av, wv], 2)),
                         merge, cols(g["w_out"]), cols(g["w_peer_q"])], 1).reshape(DEPTH * LOADS * P, SLOT_W)

    def pt(a):
        return a.reshape(DEPTH, -1, P).transpose(2, 0, 1)

    cw = g["conv_dw"].reshape(DEPTH, TAPS, CJ, P).transpose(3, 0, 2, 1).reshape(P, DEPTH, -1)
    ppd = np.concatenate([pt(g["norm1_g"]), pt(g["norm2_g"]), pt(g["b_ada"]), pt(g["b_gate"].reshape(DEPTH, -1)), cw,
                          pt(g["conv_b"]), pt(g["conv_ln_g"]), pt(g["conv_ln_b"])], 2).reshape(P, -1)
    cvec = np.stack([g["c_ctx"], g["c"][0]], 1).reshape(KD, P, 2).transpose(1, 0, 2).reshape(P, -1)
    rowd = np.concatenate([g["q_norm_g"], g["k_norm_g"], g["win_sink"]], 1)
    skd = g["peer_subkeys"].transpose(0, 3, 1, 2).reshape(DEPTH * P, 2 * P)
    kcd = np.stack([g["cache_attn_k"][0], g["cache_win_k"][0]], 1).transpose(0, 1, 4, 3, 2).reshape(DEPTH * 2 * HD, KVH * P)
    vcd = np.concatenate([g["cache_attn_v"][0].reshape(DEPTH * P, P), g["cache_win_v"][0].reshape(DEPTH * P, P)], 1)
    xin = np.concatenate([g["x_prompt"][0], g["x_sample"][0]], 0)
    cst, tab, mask = shape_constants()
    arrays = dict(ws=ws, cst=cst, tabs=tab, masks=mask, ppd=ppd, cvec=cvec, rowd=rowd, fing=g["final_norm_g"], skd=skd,
                  kcd=kcd, vcd=vcd, tables_u=g["peer_u"].reshape(-1, D), tables_v=g["peer_v"].reshape(-1, D), xin=xin)
    arrays = {k: np.ascontiguousarray(a) for k, a in arrays.items()}
    nc = bacc.Bacc("TRN2", target_bir_lowering=False, num_devices=1)
    args = [nc.dram_tensor(k, a.shape, F32, kind="ExternalInput").ap() for k, a in arrays.items()]
    y = nc.dram_tensor("y", (TOK, D), F32, kind="ExternalOutput").ap()
    nk = nc.dram_tensor("nk", (4 * DEPTH * P, P), F32, kind="ExternalOutput").ap()
    program(nc, *args, y, nk)
    r = run(nc, [arrays], core_ids=[0]).results[0]
    y, nk = r["y"], r["nk"].reshape(4, 1, DEPTH, P, KVH, HD)
    return y[None, :P], y[None, P:], nk[0], nk[1], nk[2], nk[3]
```

```python
from contextlib import ExitStack

import numpy as np
import concourse.bass as bass
from concourse import mybir

F32 = mybir.dt.float32
I32 = mybir.dt.int32
U32 = mybir.dt.uint32
ALU = mybir.AluOpType
ACT = mybir.ActivationFunctionType
AX = mybir.AxisListType

P = 128
D = 1024
DEPTH = 2
KD = D // P
TILES = 5
TOK = TILES * P
LAT = TOK - P
HALF = TOK // 2
HEADS, KVH, HD = 8, 2, 64
GROUP = HEADS // KVH
UNITS = 2 * HEADS
TAPS = 31
PAD = TAPS // 2
CONV = 512
CJ = CONV // P
SPAN = P + 2 * PAD + LAT
CPAD = SPAN + 2 * PAD
EXPERTS = 16384
PH = 8
TOPK = 16
SLOTS = PH * TOPK
EPS = 1e-6
SCALE = HD ** -0.5
NEG = -1e30 / SCALE

N_MOD, N_CP, N_QP, N_MG, N_OP, N_PQ = 24, 4, 8, 32, 4, 8
AT_CP = N_MOD
AT_QP = AT_CP + N_CP
AT_MG = AT_QP + N_QP
AT_OP = AT_MG + N_MG
AT_PQ = AT_OP + N_OP
LOADS = AT_PQ + N_PQ
WS = 4
SLOT_W = 2048

RING = 16
GROUPS = SLOTS // RING
V_DVE = [b for b in range(RING) if b % 3 == 0]
V_PE = [b for b in range(RING) if b % 3]
DVE_U = SLOTS
DVE_TILE = SLOTS + GROUPS * len(V_DVE)
PE_TILE = GROUPS * len(V_PE)

PP = {}
_o = 0
for _n, _w in (("n1", KD), ("n2", KD), ("bada", 48), ("bg", 32), ("cw", CJ * TAPS), ("cb", CJ), ("lg", CJ), ("lb", CJ)):
    PP[_n] = (_o, _w)
    _o += _w
PPW = _o


class Sig:

    def __init__(self, sem, per, first):
        self.sem, self.per, self.first = sem, per, first

    def at(self, layer, n):
        return layer * self.per + (n + self.first)


class Small:

    def __init__(self, a):
        self.hs = a[:, 0:256]
        self.cand = a[:, 256:512]
        self.EQ = a[:, 512:1024].rearrange("p (c k a) -> p c k a", c=2, k=TOPK)
        self.sv = a[:, 1024:1056].rearrange("p (c k) -> p c k", c=2)
        self.si = a[:, 1056:1088].bitcast(U32).rearrange("p (c k) -> p c k", c=2)
        self.sf = a[:, 1088:1120].rearrange("p (c k) -> p c k", c=2)
        self.tv = a[:, 1120:1136]
        self.ti = a[:, 1136:1152].bitcast(U32)
        self.pu = a[:, 1152:1184].bitcast(U32).rearrange("p (c k) -> p c k", c=2)
        self.pf = a[:, 1184:1216].rearrange("p (c k) -> p c k", c=2)
        self.ef = a[:, 1216:1248].rearrange("p (c k) -> p c k", c=2)
        self.er = a[:, 1248:1264]


SMALL = 1264


def program(nc, ws, cst, tabs, masks, ppd, cvec, rowd, fing, skd, kcd, vcd, tables_u, tables_v, xin,
            y_out, nk_out):
    with ExitStack() as ctx:
        def sb(name, shape, dt=F32):
            return ctx.enter_context(nc.sbuf_tensor(name, shape, dt))

        def sig(name, per=1, first=0):
            return Sig(ctx.enter_context(nc.semaphore(name)), per, first)

        x = sb("x", [P, TILES, D])
        hT = sb("hT", [P, KD, TOK])
        A = sb("A", [P, 2560 + 1792 + 6400])
        Fin = A[:, 0:2560].rearrange("p (t n) -> p t n", t=TILES)
        V = A[:, 2560:4352].rearrange("p (b n) -> p b n", b=7)
        TM = A[:, 4352:10752].rearrange("p (t n) -> p t n", t=TILES)
        SC = A[:, 0:10240].rearrange("p (t h k) -> p t h k", t=TILES, h=UNITS)
        M = sb("M", [P, TILES * D])
        convh = M[:, 0:CJ * CPAD].rearrange("p (j n) -> p j n", j=CJ)
        SQ = M[:, 0:CJ * SPAN].rearrange("p (j n) -> p j n", j=CJ)
        G = M[:, 2880:4160].rearrange("p (c n) -> p c n", c=2)
        RSTD = M[:, 4192:4192 + SPAN]
        Pb = [M[:, i * 640:(i + 1) * 640] for i in range(2)]
        PT = [M[:, 1280 + i * 640:1280 + (i + 1) * 640] for i in range(2)]
        MK = M[:, 2560:3584]
        QO = M[:, 3584:4608]
        mT = M[:, :].rearrange("p (k n) -> p k n", k=KD)
        h2 = M[:, :].rearrange("p (t n) -> p t n", t=TILES)
        B = sb("B", [P, 10240 + WS * SLOT_W])
        BR = B[:, 0:10240].rearrange("p (b j n) -> p b j n", b=4, j=CJ)
        YC = B[:, 5120:5120 + CJ * SPAN].rearrange("p (j n) -> p j n", j=CJ)
        Wt = [B[:, 10240 + s * SLOT_W:10240 + (s + 1) * SLOT_W] for s in range(WS)]
        XS = [B[:, 0:1024], B[:, 1024:2048]]
        JX = B[:, 3584:4608]
        AR = B[:, 0:6 * 256]
        QS = [B[:, 2048 + i * 640:2048 + (i + 1) * 640] for i in range(2)]
        ring = [B[:, i * 1024:(i + 1) * 1024] for i in range(RING)]
        junk = [B[:, (RING + i) * 1024:(RING + i + 1) * 1024] for i in range(2)]
        R = sb("R", [P, 5376])
        CS = R[:, 0:4096].rearrange("p (c t n) -> p c t n", c=2, t=4)
        C1, S1 = R[:, 4096:4224], R[:, 4224:4352]
        qT = R[0:64, 0:2048].rearrange("p (u n) -> p u n", u=UNITS)
        kTa = R[0:64, 2048:3584].rearrange("p (v n) -> p v n", v=KVH)
        kTw = R[0:64, 3584:5376].rearrange("p (v n) -> p v n", v=KVH)
        nrm = [R[:, 4400 + i * 50:4450 + i * 50] for i in range(3)]
        grow = R[:, 0:4096].rearrange("p (v s n) -> p v s n", v=2, s=2)
        EI = R[:, 4096:4096 + TILES * SLOTS].bitcast(I32)
        GT = R[:, 4736:4736 + TILES * SLOTS]
        T = sb("T", [P, 640])
        QN = [T[:, 0:512], M[:, 4608:5120]]
        SG = [TM[:, 0, 0:640], TM[:, 0, 640:1280]]
        PR = TM[:, 1, 0:640]
        hf = hT[:, :, :].rearrange("p k n -> p (k n)")
        acc = [hf[:, 0:1024], hf[:, 1024:2048]]
        early, steady = Small(B[:, 8192:8192 + SMALL]), Small(hf[:, 2048:2048 + SMALL])
        diag = [hf[:, 3840 + i * P:3840 + (i + 1) * P] for i in range(len(V_PE))]
        ew = T[:, 0:SLOTS]
        dots = T[:, SLOTS:2 * SLOTS]
        st_idx = [sb(f"st_idx{i}", [P, RING], I32) for i in range(2)]
        cs = sb("cs", [P, 4, P])
        ident, onesD, BC, BSn = [cs[:, i, :] for i in range(4)]
        rope = sb("rope", [P, 2, 4, HD])
        io = sb("io", [P, 2 * TOPK + DEPTH])
        pp = sb("pp", [P, DEPTH, PPW])
        cT = sb("cT", [P, KD, 32])
        row = sb("row", [P, DEPTH, 2 * HD + HEADS])
        nsink = sb("nsink", [P, HEADS])
        skT = sb("skT", [P, 2, P])
        wgt = skT[:, 0, :]
        adaT = sb("adaT", [P, 48, 2])
        aff = sb("aff", [P, 2, 4, KD])
        s1 = sb("s1", [P, 4 * TILES])
        sm = sb("sm", [P, 8, 2])

        ps = ctx.enter_context(nc.psum_tensor("ps", [P, 8, 512], F32))

        cst_in = sig("cst_in")
        layer_done = sig("layer_done", 1, 1)
        w_in = [sig(f"w_in{s}", 16 * LOADS // WS) for s in range(WS)]
        w_used = sig("w_used", LOADS, WS)
        c_pad = sig("c_pad")
        silu_c = sig("silu_c")
        mod_ev = sig("mod_ev")
        mod_t = sig("mod_t")
        aff_ok = sig("aff_ok", 1)
        n_ssq = sig("n_ssq", 2)
        n_sq = sig("n_sq", 2)
        n_xs = sig("n_xs", 2 * TILES)
        n_tp = sig("n_tp", 2 * TILES)
        n_ht = sig("n_ht", 2 * TILES)
        pads = sig("pads", 2)
        cp_sg = sig("cp_sg", CJ)
        cp_ev = sig("cp_ev", CJ, 2)
        qp_ps = sig("qp_ps", N_QP * (TILES - 1))
        qp_ev = sig("qp_ev", N_QP * TILES, 4)
        tab_in = sig("tab_in", 16)
        fo_ps = sig("fo_ps", CJ)
        fo_g = sig("fo_g", CJ, 1)
        fo_ops = sig("fo_ops", CJ)
        fo_o = sig("fo_o", CJ, 1)
        cv_y = sig("cv_y", 1)
        ln_mp = sig("ln_mp", 1)
        ln_d = sig("ln_d", 1)
        ln_sq = sig("ln_sq", 1)
        ln_vp = sig("ln_vp", 1)
        ln_v = sig("ln_v", 1)
        ln_sr = sig("ln_sr", 1)
        ln_n = sig("ln_n", 1)
        ln_o = sig("ln_o", 1)
        kq_s = sig("kq_s", 1)
        kq_r = sig("kq_r", 1)
        kq_ok = sig("kq_ok", 1)
        kt_ps = sig("kt_ps", 1)
        kt_ev = sig("kt_ev", 1)
        kv_in = sig("kv_in", 16 * 4)
        qs_ok = sig("qs_ok", TILES)
        qt_ps = sig("qt_ps", TILES)
        qt_a = sig("qt_a", TILES)
        qt_d = sig("qt_d", TILES)
        a_s = sig("a_s", UNITS * TILES)
        a_m = sig("a_m", UNITS * TILES)
        a_exp = sig("a_exp", UNITS * TILES, 2)
        a_t = sig("a_t", UNITS * TILES)
        a_pa = sig("a_pa", UNITS * TILES, 1)
        a_pd = sig("a_pd", UNITS * TILES, 1)
        a_o = sig("a_o", UNITS * TILES)
        a_on = sig("a_on", UNITS * TILES, 2)
        ot_ps = sig("ot_ps", TILES)
        ot_ev = sig("ot_ev", TILES, 1)
        rw_dg = sig("rw_dg", 8)
        rw_ps = sig("rw_ps", 8)
        rw_ev = sig("rw_ev", 8, 2)
        mg_g = sig("mg_g", N_MG)
        mg_sg = sig("mg_sg", N_MG)
        mg_ev = sig("mg_ev", N_MG, 2)
        mg_m = sig("mg_m", KD)
        op_ps = sig("op_ps", TILES - 1)
        op_x = sig("op_x", TILES)
        h2_ps = sig("h2_ps", TILES)
        h2_ev = sig("h2_ev", TILES)
        sk_in = sig("sk_in", 16)
        pq_ps = sig("pq_ps", UNITS // 2)
        pq_q = sig("pq_q", UNITS)
        pq_sp = sig("pq_sp", UNITS)
        pq_s = sig("pq_s", UNITS, 2)
        ei_ok = sig("ei_ok", TILES * PH)
        st_ok = sig("st_ok", TILES * 2 * GROUPS)
        got = [sig(f"got{b}", 16 * TILES * 2 * GROUPS) for b in range(RING)]
        dve_used = sig("dve_used", TILES * DVE_TILE, len(V_DVE))
        pe_used = sig("pe_used", TILES * PE_TILE, len(V_PE))
        early_ok = sig("early_ok", 1)
        wgt_ok = sig("wgt_ok", TILES)
        diag_ok = sig("diag_ok", TILES * PE_TILE)
        pool_go = sig("pool_go")
        pe_go = sig("pe_go")
        dve_go = sig("dve_go")
        act_go = sig("act_go")
        u_done = sig("u_done", TILES)
        u_act = sig("u_act", TILES)
        nk_done = sig("nk_done", 16 * 4)
        f_g = sig("f_g")
        f_ss = sig("f_ss")
        f_sq = sig("f_sq")
        f_y = sig("f_y")
        out_done = sig("out_done")

        block = ctx.enter_context(nc.Block())

        @block.sync
        def _(sp):
            for dst, src in ((x[:, :, :], xin.rearrange("(t p) n -> p t n", p=P)),
                             (cs[:, :, :], cst[:, 0:512].rearrange("p (c n) -> p c n", c=4)),
                             (rope[:, :, :, :], cst[:, 512:1024].rearrange("p (c t n) -> p c t n", c=2, t=4)),
                             (io[:, :], cst[:, 1024:1024 + 2 * TOPK + DEPTH]),
                             (pp[:, :, :], ppd.rearrange("p (l n) -> p l n", l=DEPTH)),
                             (cT[:, :, 0:2], cvec.rearrange("p (k s) -> p k s", k=KD)),
                             (row[:, :, :], rowd.partition_broadcast(P))):
                sp.dma_start(dst, src).then_inc(cst_in.sem, 16)
            with sp.Fori(0, DEPTH) as l:
                sp.wait_ge(layer_done.sem, layer_done.at(l, 0))
                sp.dma_start(R[:, 0:4352], tabs[:, :]).then_inc(tab_in.sem, 16)
                sp.dma_start(skT[:, :, :], skd[bass.ds(l * P, P), :].rearrange("p (c n) -> p c n", c=2))\
                    .then_inc(sk_in.sem, 16)

                def load(n, s, width):
                    sp.wait_ge(w_used.sem, w_used.at(l, n + 1 - WS))
                    sp.dma_start(Wt[s][:, 0:width], ws[bass.ds((l * LOADS + n) * P, P), 0:width])\
                        .then_inc(w_in[s].sem, 16)

                with sp.Fori(0, AT_MG // WS) as q:
                    for s in range(WS):
                        load(q * WS + s, s, SLOT_W)
                sp.wait_ge(fo_ops.sem, fo_ops.at(l, CJ))
                sp.wait_ge(ln_o.sem, ln_o.at(l, 1))
                sp.dma_start(MK, masks[:, :]).then_inc(kv_in.sem, 16)
                sp.dma_start(kTa[:, :, 4 * P:5 * P], kcd[bass.ds(l * 2 * HD, HD), :]
                             .rearrange("p (v n) -> p v n", v=KVH)).then_inc(kv_in.sem, 16)
                sp.dma_start(kTw[:, :, 6 * P:7 * P], kcd[bass.ds(l * 2 * HD + HD, HD), :]
                             .rearrange("p (v n) -> p v n", v=KVH)).then_inc(kv_in.sem, 16)
                sp.dma_start(V[:, 6, :], vcd[bass.ds(l * P, P), :]).then_inc(kv_in.sem, 16)
                sp.wait_ge(kq_ok.sem, kq_ok.at(l, 1))
                for i, src in enumerate((TM[:, 0, 512:640], V[:, 0, 0:128], TM[:, 0, 1152:1280], V[:, 0, 128:256])):
                    sp.dma_start(nk_out[bass.ds((l + i * DEPTH) * P, P), :], src).then_inc(nk_done.sem, 16)
                with sp.Fori(AT_MG // WS, AT_OP // WS) as q:
                    for s in range(WS):
                        load(q * WS + s, s, 12 * P)
                with sp.Fori(AT_OP // WS, LOADS // WS) as q:
                    for s in range(WS):
                        load(q * WS + s, s, SLOT_W)
            sp.wait_ge(layer_done.sem, DEPTH + 1)
            sp.dma_start(R[:, 0:D], fing.partition_broadcast(P)).then_inc(f_g.sem, 16)
            sp.wait_ge(f_y.sem, TILES)
            sp.dma_start(y_out.rearrange("(t p) n -> p t n", p=P), h2).then_inc(out_done.sem, 16)
            sp.wait_ge(out_done.sem, 16)
            sp.wait_ge(nk_done.sem, 64 * DEPTH)

        @block.gpsimd
        def _(pool):
            with pool.Fori(0, DEPTH) as l:
                pool.wait_ge(layer_done.sem, layer_done.at(l, 0))
                pool.sem_inc(pool_go.sem, 1)
                pool.memset(convh, 0.0)
                pool.memset(V[:, 5, :], 0.0).then_inc(pads.sem, 1)
                pool.wait_ge(fo_ops.sem, fo_ops.at(l, CJ))
                pool.sem_inc(pool_go.sem, 1)
                pool.memset(kTw[:, :, 5 * P:6 * P], 0.0).then_inc(pads.sem, 1)

                def queries(n):
                    flat = A[:, 4352:10752]
                    pool.tensor_copy(QN[0], flat[:, bass.ds(n * 1280 + 640, 512)])
                    pool.tensor_copy(QN[1], flat[:, bass.ds(n * 1280, 512)]).then_inc(qs_ok.sem, 1)

                pool.wait_ge(kq_ok.sem, kq_ok.at(l, 1))
                pool.wait_ge(ln_n.sem, ln_n.at(l, 1))
                pool.sem_inc(pool_go.sem, 1)
                queries(0)
                with pool.Fori(1, TILES) as n:
                    pool.wait_ge(qt_ps.sem, qt_ps.at(l, n))
                    pool.sem_inc(pool_go.sem, 1)
                    queries(n)
                pool.wait_ge(pq_s.sem, pq_s.at(l, UNITS))
                pool.sem_inc(pool_go.sem, 1)

                def before_used(t, uv, g, b):
                    if uv == 0 and isinstance(g, int) and g == 0:
                        t, uv, g = t - 1, 1, GROUPS
                    if uv == 0 or isinstance(g, int) and g == 0:
                        pool.wait_ge(dve_used.sem, dve_used.at(l, t * DVE_TILE + (g + uv * GROUPS) * RING + b + 1 - RING))
                    elif b in V_DVE:
                        pool.wait_ge(dve_used.sem, dve_used.at(l, t * DVE_TILE + g * len(V_DVE)
                                                               + (DVE_U - len(V_DVE) + V_DVE.index(b) + 1)))
                    else:
                        pool.wait_ge(pe_used.sem, pe_used.at(l, t * PE_TILE + g * len(V_PE)
                                                             + (V_PE.index(b) + 1 - len(V_PE))))
                    pool.sem_inc(pool_go.sem, 1)

                def gather_group(t, uv, g, half):
                    pool.wait_ge(ei_ok.sem, ei_ok.at(l, t * PH + (g + 1)))
                    pool.sem_inc(pool_go.sem, 1)
                    pool.tensor_copy(st_idx[half][:, :], EI[:, bass.ds(t * SLOTS + g * RING, RING)]).then_inc(st_ok.sem, 1)
                    pool.wait_ge(st_ok.sem, st_ok.at(l, (t * 2 + uv) * GROUPS + g + 1))
                    pool.sem_inc(pool_go.sem, 1)
                    for b in range(RING):
                        before_used(t, uv, g, b)
                        if b == 8 and uv == 0 and isinstance(g, int) and g == 0:
                            pool.wait_ge(early_ok.sem, early_ok.at(l, 1))
                            pool.sem_inc(pool_go.sem, 1)
                        pool.indirect_dma_start(
                            out=ring[b], out_offset=None, in_=(tables_u, tables_v)[uv][:, :],
                            in_offset=bass.IndirectOffsetOnAxis(ap=st_idx[half][:, b:b + 1], axis=0),
                        ).then_inc(got[b].sem, 16)

                with pool.Fori(0, TILES) as t:
                    for uv in range(2):
                        for g in range(2):
                            gather_group(t, uv, g, g)
                        with pool.Fori(1, GROUPS // 2) as q:
                            for half in range(2):
                                gather_group(t, uv, q * 2 + half, half)

        @block.tensor
        def _(pe):
            def arrived(l, n, s):
                pe.wait_ge(w_in[s].sem, w_in[s].at(l, (n + 1) * 16))

            def norm_transposes(l, first):
                for t in range(TILES):
                    bk = 4 + (t % 2) * 2
                    pe.wait_ge(n_xs.sem, n_xs.at(l, first + t + 1))
                    if t >= 2:
                        pe.wait_ge(n_ht.sem, n_ht.at(l, first + t - 1))
                    for k in range(KD):
                        last = pe.transpose(ps[:, bk + k // 4, (k % 4) * P:(k % 4 + 1) * P], XS[t % 2][:, k * P:(k + 1) * P], ident)
                    last.then_inc(n_tp.sem, 1)

            pe.sem_inc(w_used.sem, WS)
            pe.wait_ge(silu_c.sem, 1)
            pe.wait_ge(c_pad.sem, 1)
            psm = ps[:, :, :].rearrange("p b n -> p (b n)")
            with pe.Fori(0, DEPTH) as l:
                pe.wait_ge(layer_done.sem, layer_done.at(l, 0))
                pe.sem_inc(pe_go.sem, 1)
                for q in range(N_MOD // WS):
                    for s0 in (0, 2):
                        for s in (s0, s0 + 1):
                            arrived(l, q, s)
                        for k in range(KD):
                            for s in (s0, s0 + 1):
                                last = pe.matmul(psm[32 * s:32 * s + 32, q * 256:(q + 1) * 256], cT[:, k, :],
                                                 Wt[s][:, k * 256:(k + 1) * 256], start=(k == 0), stop=(k == KD - 1))
                                if k == KD - 1:
                                    last.then_inc(w_used.sem, 1)
                pe.wait_ge(mod_ev.sem, mod_ev.at(l, 1))
                for m in range(2 * N_MOD // WS):
                    last = pe.transpose(ps[:, 4 + m // 4, (m % 4) * P:(m % 4 + 1) * P], AR[:, m * P:(m + 1) * P], ident)
                last.then_inc(mod_t.sem, 1)
                pe.wait_ge(aff_ok.sem, aff_ok.at(l, 1))
                norm_transposes(l, 0)

                pe.wait_ge(n_ht.sem, n_ht.at(l, TILES))
                for j in range(CJ):
                    arrived(l, AT_CP // WS, j)
                    pe.wait_ge(cp_ev.sem, cp_ev.at(l, j + 1 - 2))
                    bk = (j % 2) * 4
                    for c in range(2):
                        for bank, lo, hi in ((0, P, TOK), (1, 0, P)):
                            for k in range(KD):
                                last = pe.matmul(ps[:, bk + 2 * c + bank, 0:hi - lo],
                                                 Wt[j][:, k * 256 + c * P:k * 256 + c * P + P], hT[:, k, lo:hi],
                                                 start=(k == 0), stop=(k == KD - 1))
                    last.then_inc(w_used.sem, 1)

                pe.wait_ge(cp_ev.sem, cp_ev.at(l, CJ))
                pe.sem_inc(pe_go.sem, 1)
                with pe.Fori(0, N_QP // WS) as q:
                    for s in range(WS):
                        arrived(l, q + AT_QP // WS, s)
                        for t in range(TILES):
                            g = s * TILES + t
                            pe.wait_ge(qp_ev.sem, qp_ev.at(l, q * WS * TILES + g + 1 - 4))
                            for k in range(KD):
                                last = pe.matmul(ps[:, g % 4, 0:256], hT[:, k, t * P:(t + 1) * P],
                                                 Wt[s][:, k * 256:(k + 1) * 256], start=(k == 0), stop=(k == KD - 1))
                            last.then_inc(qp_ps.sem if t < TILES - 1 else w_used.sem, 1)

                pe.wait_ge(qp_ev.sem, qp_ev.at(l, N_QP * TILES))
                pe.wait_ge(tab_in.sem, tab_in.at(l, 16))
                h = SPAN // 2

                def channel_means(src, bank0):
                    for bank in range(2):
                        for j in range(CJ):
                            last = pe.matmul(ps[:, bank0 + bank, 0:h], onesD, src[:, j, bank * h:(bank + 1) * h],
                                             start=(j == 0), stop=(j == CJ - 1))
                    return last

                pe.wait_ge(cv_y.sem, cv_y.at(l, 1))
                channel_means(YC, 2).then_inc(ln_mp.sem, 1)
                for j in range(CJ):
                    if j == 2:
                        pe.wait_ge(ln_sq.sem, ln_sq.at(l, 1))
                        channel_means(SQ, 2).then_inc(ln_vp.sem, 1)
                    pe.wait_ge(fo_g.sem, fo_g.at(l, j))
                    cols = slice(j * P, (j + 1) * P)
                    for c, tab in enumerate((C1, S1)):
                        for t in range(4):
                            pe.matmul(ps[:, 4 + 2 * c, :], Fin[:, t + 1, cols], CS[:, c, t, :], start=(t == 0), stop=(t == 3))
                        last = pe.matmul(ps[:, 5 + 2 * c, 0:P], Fin[:, 0, cols], tab, start=True, stop=True)
                    last.then_inc(fo_ps.sem, 1)
                    pe.wait_ge(fo_g.sem, fo_g.at(l, j + 1))
                    pe.wait_ge(fo_o.sem, fo_o.at(l, j))
                    for bank, lo, hi in ((0, P, TOK), (1, 0, P)):
                        pe.matmul(ps[:, bank, 0:hi - lo], BC, G[:, 0, lo:hi], start=True, stop=False)
                        last = pe.matmul(ps[:, bank, 0:hi - lo], BSn, G[:, 1, lo:hi], start=False, stop=True)
                    last.then_inc(fo_ops.sem, 1)

                pe.wait_ge(fo_o.sem, fo_o.at(l, CJ))
                pe.wait_ge(ln_v.sem, ln_v.at(l, 1))
                pe.wait_ge(kq_ok.sem, kq_ok.at(l, 1))
                pe.sem_inc(pe_go.sem, 1)
                for t in range(TILES):
                    for i, c in enumerate((512, 576, 1152, 1216)):
                        last = pe.transpose(ps[0:HD, t, i * P:(i + 1) * P], TM[:, t, c:c + HD], ident)
                last.then_inc(kt_ps.sem, 1)
                pe.wait_ge(kt_ev.sem, kt_ev.at(l, 1))

                def attention(n, t):
                    u0 = n * UNITS
                    pe.wait_ge(qs_ok.sem, qs_ok.at(l, n + 1))
                    pe.wait_ge(a_exp.sem, a_exp.at(l, u0))
                    pe.sem_inc(pe_go.sem, 1)
                    for u in range(UNITS):
                        last = pe.transpose(ps[0:HD, u // 4, (u % 4) * P:(u % 4 + 1) * P],
                                            QN[u // HEADS][:, (u % HEADS) * HD:(u % HEADS + 1) * HD], ident)
                    last.then_inc(qt_ps.sem, 1)
                    pe.wait_ge(qt_a.sem, qt_a.at(l, n + 1))
                    pe.wait_ge(qt_d.sem, qt_d.at(l, n + 1))

                    def scores(u):
                        pe.wait_ge(a_exp.sem, a_exp.at(l, u0 + u - 1))
                        pe.sem_inc(pe_go.sem, 1)
                        q, bk, kv = qT[:, u, :], (u % 2) * 2, (u % HEADS) // GROUP
                        if t is None:
                            keys = kTw[:, kv, 0:P] if windowed(u) else kTa[:, kv, 5 * P:6 * P]
                            last = pe.matmul(ps[:, bk, 0:P], q, keys, start=True, stop=True)
                        elif not windowed(u):
                            for i in range(2):
                                last = pe.matmul(ps[:, bk + i, 0:HALF], q, kTa[:, kv, i * HALF:(i + 1) * HALF],
                                                 start=True, stop=True)
                        else:
                            pe.matmul(ps[:, bk, 0:3 * P], q, kTw[:, kv, bass.ds(t * P, 3 * P)], start=True, stop=False)
                            pe.matmul(ps[:, bk, :].rearrange("p (a c n) -> p a c n", a=2, c=2)[:, :, 0, :], ident,
                                      MK[:, bass.ds(t * 2 * P, 2 * P)].rearrange("p (a n) -> p a n", a=2), start=False, stop=True)
                            last = pe.matmul(ps[:, bk, 3 * P:4 * P], q, kTw[:, kv, 6 * P:7 * P], start=True, stop=True)
                        last.then_inc(a_s.sem, 1)

                    def transpose_part(u, i):
                        split = dve_blocks(t, u)
                        bank, o = (4, i) if i < split else (5, i - split)
                        return pe.transpose(ps[:, bank, o * P:(o + 1) * P], Pb[u % 2][:, i * P:(i + 1) * P], ident)

                    def value_part(u, i):
                        c = (u % HEADS) // GROUP * HD + windowed(u) * P
                        if t is None:
                            values = V[:, 0, c:c + HD]
                        elif not windowed(u):
                            values = V[:, (1, 2, 3, 4, 6)[i], c:c + HD]
                        elif i < 3:
                            values = A[:, 2560:4352][:, bass.ds((t + i) * 256 + c, HD)]
                        else:
                            values = V[:, 6, c:c + HD]
                        return pe.matmul(ps[:, 6 + u % 2, 0:HD], PT[u % 2][:, i * P:(i + 1) * P], values,
                                         start=(i == 0), stop=(i == blocks(t, u) - 1))

                    def transposes_and_values(u):
                        nt = blocks(t, u) if u < UNITS else 0
                        nv = blocks(t, u - 1) if u else 0
                        if nt:
                            pe.wait_ge(a_exp.sem, a_exp.at(l, u0 + u + 1))
                        pe.wait_ge(a_pa.sem, a_pa.at(l, u0 + u))
                        pe.wait_ge(a_pd.sem, a_pd.at(l, u0 + u))
                        if nt and u < 2:
                            pe.wait_ge(ot_ev.sem, ot_ev.at(l, n))
                        if nv:
                            pe.wait_ge(a_on.sem, a_on.at(l, u0 + u - 2))
                        pe.sem_inc(pe_go.sem, 1)
                        for i in range(max(nt, nv)):
                            if i < nt:
                                last = transpose_part(u, i)
                                if i == nt - 1:
                                    last.then_inc(a_t.sem, 1)
                            if i < nv:
                                last = value_part(u - 1, i)
                                if i == nv - 1:
                                    last.then_inc(a_o.sem, 1)

                    for u in range(UNITS + 2):
                        if u < UNITS:
                            scores(u)
                        if u:
                            transposes_and_values(u - 1)
                    pe.wait_ge(a_on.sem, a_on.at(l, u0 + UNITS))
                    for i in range(8):
                        last = pe.transpose(ps[:, 4 + i // 4, (i % 4) * P:(i % 4 + 1) * P], QO[:, i * P:(i + 1) * P], ident)
                    last.then_inc(ot_ps.sem, 1)

                attention(0, None)
                pe.wait_ge(kv_in.sem, kv_in.at(l, 64))
                pe.wait_ge(pads.sem, pads.at(l, 2))
                pe.sem_inc(pe_go.sem, 1)
                with pe.Fori(0, TILES - 1) as t:
                    attention(t + 1, t)

                for i in range(8):
                    pe.wait_ge(rw_dg.sem, rw_dg.at(l, i + 1))
                    pe.wait_ge(rw_ev.sem, rw_ev.at(l, i - 1))
                    pe.matmul(ps[:, i % 2, :], onesD, T[:, 0:512], start=True, stop=True).then_inc(rw_ps.sem, 1)

                pe.wait_ge(rw_ev.sem, rw_ev.at(l, 8))
                pe.wait_ge(ot_ev.sem, ot_ev.at(l, TILES))
                pe.wait_ge(ln_o.sem, ln_o.at(l, 1))
                pe.sem_inc(pe_go.sem, 1)
                with pe.Fori(0, KD) as j:
                    for b in range(4):
                        arrived(l, j + AT_MG // WS, b)
                        bk = (b % 2) * 4
                        pe.wait_ge(mg_ev.sem, mg_ev.at(l, j * 4 + b - 1))
                        for i in range(2):
                            for k in range(KD):
                                last = pe.matmul(ps[:, bk + i, 0:HALF], Wt[b][:, k * P:(k + 1) * P],
                                                 hT[:, k, i * HALF:(i + 1) * HALF], start=(k == 0), stop=(k == KD - 1))
                        last.then_inc(mg_g.sem, 1)
                        for i in range(2):
                            for k in range(CJ):
                                last = pe.matmul(ps[:, bk + 2 + i, 0:HALF], Wt[b][:, (KD + k) * P:(KD + k + 1) * P],
                                                 BR[:, b, k, i * HALF:(i + 1) * HALF], start=(k == 0), stop=(k == CJ - 1))
                        last.then_inc(w_used.sem, 1)

                pe.wait_ge(mg_m.sem, mg_m.at(l, KD))
                for s in range(WS):
                    arrived(l, AT_OP // WS, s)
                for t in range(TILES):
                    bk = (t % 4) * 2
                    if t >= 4:
                        pe.wait_ge(op_x.sem, op_x.at(l, t - 3))
                    for c in range(4):
                        for k in range(KD):
                            last = pe.matmul(ps[:, bk + c // 2, (c % 2) * 256:(c % 2 + 1) * 256], mT[:, k, t * P:(t + 1) * P],
                                             Wt[c][:, k * 256:(k + 1) * 256], start=(k == 0), stop=(k == KD - 1))
                        if t == TILES - 1:
                            last.then_inc(w_used.sem, 1)
                    if t < TILES - 1:
                        last.then_inc(op_ps.sem, 1)

                norm_transposes(l, TILES)
                pe.wait_ge(n_ht.sem, n_ht.at(l, 2 * TILES))
                for t in range(TILES):
                    bk = (t % 2) * 2
                    if t >= 2:
                        pe.wait_ge(h2_ev.sem, h2_ev.at(l, t - 1))
                    for k in range(KD):
                        last = pe.transpose(ps[:, bk + k // 4, (k % 4) * P:(k % 4 + 1) * P], hT[:, k, t * P:(t + 1) * P], ident)
                    last.then_inc(h2_ps.sem, 1)

                pe.wait_ge(h2_ev.sem, h2_ev.at(l, TILES))
                pe.wait_ge(sk_in.sem, sk_in.at(l, 16))
                pe.sem_inc(pe_go.sem, 1)
                with pe.Fori(0, N_PQ // WS) as q:
                    def key_scores(i):
                        hp = q * 8 + i
                        pe.wait_ge(pq_q.sem, pq_q.at(l, hp + 1))
                        pe.wait_ge(pq_s.sem, pq_s.at(l, hp - 1))
                        for t in range(TILES):
                            last = pe.matmul(ps[:, (i % 2) * 2 + t // 4, (t % 4) * P:(t % 4 + 1) * P],
                                             QS[i % 2][:, t * P:(t + 1) * P], skT[:, i % 2, :], start=True, stop=True)
                        last.then_inc(pq_sp.sem, 1)

                    for i in range(8):
                        s = i // 2
                        if i % 2 == 0:
                            arrived(l, q + AT_PQ // WS, s)
                        for b in range(2):
                            for k in range(KD):
                                c = k * 256 + (i % 2) * P
                                last = pe.matmul(ps[:, 4 + (i % 2) * 2 + b, 0:HALF], Wt[s][:, c:c + P],
                                                 hT[:, k, b * HALF:(b + 1) * HALF], start=(k == 0), stop=(k == KD - 1))
                        last.then_inc(w_used.sem if i % 2 else pq_ps.sem, 1)
                        if i:
                            key_scores(i - 1)
                    key_scores(7)

                def group_sums(t, g, first, last):
                    for i, b in enumerate(V_PE):
                        pe.wait_ge(diag_ok.sem, diag_ok.at(l, t * PE_TILE + g * len(V_PE) + i + 1))
                        pe.wait_ge(got[b].sem, got[b].at(l, (t * 2 * GROUPS + GROUPS + g + 1) * 16))
                        for c in range(2):
                            mm = pe.matmul(ps[:, 6 + c, :], diag[i], ring[b][:, c * 512:(c + 1) * 512],
                                           start=(first and i == 0), stop=(last and i == len(V_PE) - 1))
                        mm.then_inc(pe_used.sem, 1)

                with pe.Fori(0, TILES) as t:
                    group_sums(t, 0, True, False)
                    with pe.Fori(1, GROUPS - 1) as g:
                        group_sums(t, g, False, False)
                    group_sums(t, GROUPS - 1, False, True)

        @block.scalar
        def _(act):
            def norm(l, first, kind):
                n = first // TILES + 1
                act.wait_ge(n_ssq.sem, n_ssq.at(l, n))
                act.activation(s1[:, TILES:2 * TILES], s1[:, 0:TILES], ACT.Sqrt).then_inc(n_sq.sem, 1)
                for t in range(TILES):
                    bk = 4 + (t % 2) * 2
                    act.wait_ge(n_tp.sem, n_tp.at(l, first + t + 1))
                    for k in range(KD):
                        last = act.activation(hT[:, k, t * P:(t + 1) * P], ps[:, bk + k // 4, (k % 4) * P:(k % 4 + 1) * P],
                                              ACT.Identity, bias=aff[:, min(t, 1), 2 * kind + 1, k:k + 1],
                                              scale=aff[:, min(t, 1), 2 * kind, k:k + 1])
                    last.then_inc(n_ht.sem, 1)

            act.sem_inc(qp_ev.sem, 4)
            act.sem_inc(fo_g.sem, 1)
            act.sem_inc(fo_o.sem, 1)
            act.sem_inc(a_exp.sem, 2)
            act.sem_inc(a_pa.sem, 1)
            act.sem_inc(ot_ev.sem, 1)
            act.sem_inc(rw_ev.sem, 2)
            act.wait_ge(cst_in.sem, 7 * 16)
            act.activation(cT[:, :, 0:2], cT[:, :, 0:2], ACT.Silu).then_inc(silu_c.sem, 1)
            with act.Fori(0, DEPTH) as l:
                ppl = pp[:, :, :].rearrange("p l n -> p (l n)")

                def par(name, i):
                    return ppl[:, bass.ds(l * PPW + (PP[name][0] + i), 1)]

                act.wait_ge(aff_ok.sem, aff_ok.at(l, 1))
                norm(l, 0, 0)
                for j in range(CJ):
                    act.wait_ge(w_used.sem, w_used.at(l, AT_CP + j + 1))
                    act.wait_ge(cp_ev.sem, cp_ev.at(l, j - 1))
                    bk = (j % 2) * 4 + 2
                    act.activation(G[:, j % 2, P:TOK], ps[:, bk, :], ACT.Sigmoid)
                    act.activation(G[:, j % 2, 0:P], ps[:, bk + 1, 0:P], ACT.Sigmoid).then_inc(cp_sg.sem, 1)
                act.wait_ge(pads.sem, pads.at(l, 1))
                for c in range(N_QP):
                    for t in range(TILES):
                        g = c * TILES + t
                        if t < TILES - 1:
                            act.wait_ge(qp_ps.sem, qp_ps.at(l, c * (TILES - 1) + t + 1))
                        else:
                            act.wait_ge(w_used.sem, w_used.at(l, AT_QP + c + 1))
                        src = ps[:, g % 4, 0:256]
                        if c < 4:
                            o = (0, 256, 640, 896)[c]
                            last = act.copy(TM[:, t, o:o + 256], src)
                        elif c == 4:
                            act.copy(TM[:, t, 512:640], src[:, 0:P])
                            last = act.copy(TM[:, t, 1152:1280], src[:, P:2 * P])
                        elif c == 5:
                            last = act.copy(V[:, t, :], src)
                        else:
                            last = act.copy(Fin[:, t, (c - 6) * 256:(c - 5) * 256], src)
                        last.then_inc(qp_ev.sem, 1)
                    if c == 6:
                        act.wait_ge(kq_s.sem, kq_s.at(l, 1))
                        act.activation(nrm[1], nrm[0], ACT.Sqrt).then_inc(kq_r.sem, 1)
                act.wait_ge(cp_ev.sem, cp_ev.at(l, CJ))
                for j in range(CJ):
                    if j == 1:
                        act.wait_ge(ln_d.sem, ln_d.at(l, 1))
                        act.activation(SQ, YC, ACT.Square).then_inc(ln_sq.sem, 1)
                    if j == 3:
                        act.wait_ge(ln_v.sem, ln_v.at(l, 1))
                        act.activation(RSTD, RSTD, ACT.Sqrt).then_inc(ln_sr.sem, 1)
                    act.wait_ge(fo_ps.sem, fo_ps.at(l, j + 1))
                    if j:
                        act.wait_ge(fo_ops.sem, fo_ops.at(l, j))
                    for c in range(2):
                        act.copy(G[:, c, P:TOK], ps[:, 4 + 2 * c, :])
                        last = act.copy(G[:, c, 0:P], ps[:, 5 + 2 * c, 0:P])
                    last.then_inc(fo_g.sem, 1)
                    act.wait_ge(fo_ops.sem, fo_ops.at(l, j + 1))
                    act.copy(BR[:, 0, j, P:TOK], ps[:, 0, :])
                    act.copy(BR[:, 0, j, 0:P], ps[:, 1, 0:P]).then_inc(fo_o.sem, 1)
                act.wait_ge(ln_n.sem, ln_n.at(l, 1))
                for j in range(CJ):
                    act.activation(BR[:, 1, j, 0:P], YC[:, j, 0:P], ACT.Silu, bias=par("lb", j), scale=par("lg", j))
                    last = act.activation(BR[:, 1, j, P:TOK], YC[:, j, P + 2 * PAD:SPAN], ACT.Silu,
                                          bias=par("lb", j), scale=par("lg", j))
                last.then_inc(ln_o.sem, 1)
                act.wait_ge(kt_ps.sem, kt_ps.at(l, 1))
                for t in range(TILES):
                    blk = 5 if t == 0 else t - 1
                    act.copy(kTa[:, :, blk * P:(blk + 1) * P], ps[0:HD, t, 0:256].rearrange("p (v n) -> p v n", v=2))
                    last = act.copy(kTw[:, :, t * P:(t + 1) * P], ps[0:HD, t, 256:512].rearrange("p (v n) -> p v n", v=2))
                last.then_inc(kt_ev.sem, 1)

                def attention(n, t):
                    u0 = n * UNITS
                    act.wait_ge(qt_ps.sem, qt_ps.at(l, n + 1))
                    act.copy(qT[:, 0:8, :], ps[0:HD, 0:2, :].rearrange("p b (u n) -> p (b u) n", n=P)).then_inc(qt_a.sem, 1)

                    def exps(u):
                        act.wait_ge(a_m.sem, a_m.at(l, u0 + u + 1))
                        if u >= 2:
                            act.wait_ge(a_t.sem, a_t.at(l, u0 + u - 1))
                        bk, e = (u % 2) * 2, u % 2
                        nb = blocks(t, u)
                        if nb == 5:
                            src = ps[:, bk:bk + 2, 0:HALF]
                            dst = Pb[e].rearrange("p (i n) -> p i n", i=2)
                        else:
                            src, dst = ps[:, bk, 0:nb * P], Pb[e][:, 0:nb * P]
                        if windowed(u):
                            act.activation(sm[:, 3, e:e + 1], nsink[:, u:u + 1], ACT.Exp, bias=sm[:, 1, e:e + 1], scale=-1.0)
                        act.activation(dst, src, ACT.Exp, bias=sm[:, 1, e:e + 1], scale=SCALE,
                                       accum_out=sm[:, 2, e:e + 1]).then_inc(a_exp.sem, 1)

                    def pt_copy(u):
                        nb, split = blocks(t, u), dve_blocks(t, u)
                        if nb == split:
                            act.sem_inc(a_pa.sem, 1)
                            return
                        act.wait_ge(a_t.sem, a_t.at(l, u0 + u + 1))
                        if u >= 2:
                            act.wait_ge(a_o.sem, a_o.at(l, u0 + u - 1))
                        act.copy(PT[u % 2][:, split * P:nb * P], ps[:, 5, 0:(nb - split) * P]).then_inc(a_pa.sem, 1)

                    for u in range(UNITS + 1):
                        if u < UNITS:
                            exps(u)
                        if u:
                            pt_copy(u - 1)
                    act.wait_ge(ot_ps.sem, ot_ps.at(l, n + 1))
                    brf = B[:, 5120:10240].rearrange("p (b n) -> p b n", b=8)
                    act.copy(brf[:, 4:8, bass.ds(n * P, P)], ps[:, 4, :].rearrange("p (j n) -> p j n", n=P))
                    act.copy(brf[:, 0:4, bass.ds(n * P, P)], ps[:, 5, :].rearrange("p (j n) -> p j n", n=P))\
                        .then_inc(ot_ev.sem, 1)

                attention(0, None)
                with act.Fori(0, TILES - 1) as t:
                    attention(t + 1, t)

                for i in range(8):
                    act.wait_ge(rw_ps.sem, rw_ps.at(l, i + 1))
                    act.activation(grow[:, i // 4, (i // 2) % 2, (i % 2) * 512:(i % 2 + 1) * 512], ps[:, i % 2, :],
                                   ACT.Copy, scale=float(CONV)).then_inc(rw_ev.sem, 1)
                with act.Fori(0, KD) as j:
                    for b in range(4):
                        act.wait_ge(mg_g.sem, mg_g.at(l, j * 4 + b + 1))
                        act.wait_ge(mg_ev.sem, mg_ev.at(l, j * 4 + b - 1))
                        act.activation(SG[b % 2].rearrange("p (i n) -> p i n", i=2), ps[:, (b % 2) * 4:(b % 2) * 4 + 2, 0:HALF],
                                       ACT.Sigmoid, bias=ppl[:, bass.ds(l * PPW + j + (PP["bg"][0] + b * KD), 1)])\
                            .then_inc(mg_sg.sem, 1)
                norm(l, TILES, 1)
                for t in range(TILES):
                    act.wait_ge(h2_ps.sem, h2_ps.at(l, t + 1))
                    act.copy(h2[:, t, :].rearrange("p (b n) -> p b n", b=2), ps[:, (t % 2) * 2:(t % 2) * 2 + 2, :])\
                        .then_inc(h2_ev.sem, 1)
                with act.Fori(0, UNITS // 2) as q:
                    for i in range(2):
                        if i == 0:
                            act.wait_ge(pq_ps.sem, pq_ps.at(l, q + 1))
                        else:
                            act.wait_ge(w_used.sem, w_used.at(l, q + (AT_PQ + 1)))
                        act.wait_ge(pq_s.sem, pq_s.at(l, q * 2 + i - 1))
                        act.copy(QS[i].rearrange("p (b n) -> p b n", b=2), ps[:, 4 + 2 * i:6 + 2 * i, 0:HALF])\
                            .then_inc(pq_q.sem, 1)

                with act.Fori(0, TILES) as t:
                    act.wait_ge(u_done.sem, u_done.at(l, t + 1))
                    act.activation(ew, GT[:, bass.ds(t * SLOTS, SLOTS)], ACT.Exp)
                    act.activation(dots, dots, ACT.Gelu_apprx_tanh).then_inc(u_act.sem, 1)
                    act.wait_ge(wgt_ok.sem, wgt_ok.at(l, t + 1))
                    act.sem_inc(act_go.sem, 1)
                    with act.Fori(0, GROUPS) as g:
                        for i, b in enumerate(V_PE):
                            act.wait_ge(pe_used.sem, pe_used.at(l, t * PE_TILE + g * len(V_PE) + (i + 1 - len(V_PE))))
                            act.activation(diag[i], ident, ACT.Copy, scale=wgt[:, bass.ds(g * RING + b, 1)])\
                                .then_inc(diag_ok.sem, 1)
            act.wait_ge(f_ss.sem, 1)
            act.activation(s1[:, TILES:2 * TILES], s1[:, 0:TILES], ACT.Sqrt).then_inc(f_sq.sem, 1)

        @block.vector
        def _(v):
            def square_sum(t):
                return v.scalar_tensor_tensor(out=JX, in0=x[:, t, :], scalar=1.0, in1=x[:, t, :], op0=ALU.mult, op1=ALU.mult,
                                              accum_out=s1[:, 2 * TILES + t:2 * TILES + t + 1])

            def inverse_roots(ssq, sq, at_sq):
                v.drain()
                v.tensor_scalar(out=s1[:, 0:TILES], in0=s1[:, 2 * TILES:3 * TILES], scalar1=1.0 / D, scalar2=EPS,
                                op0=ALU.mult, op1=ALU.add).then_inc(ssq.sem, 1)
                v.wait_ge(sq.sem, at_sq)
                v.reciprocal(s1[:, 3 * TILES:4 * TILES], s1[:, TILES:2 * TILES])
                v.drain()

            def norm(l, first):
                inverse_roots(n_ssq, n_sq, n_sq.at(l, first // TILES + 1))
                for t in range(TILES):
                    if t >= 2:
                        v.wait_ge(n_tp.sem, n_tp.at(l, first + t - 1))
                    v.tensor_scalar(out=XS[t % 2], in0=x[:, t, :], scalar1=s1[:, 3 * TILES + t:3 * TILES + t + 1], scalar2=None,
                                    op0=ALU.mult).then_inc(n_xs.sem, 1)

            xf = x[:, :, :].rearrange("p t n -> p (t n)")
            v.memset(cT[:, :, 2:32], 0.0).then_inc(c_pad.sem, 1)
            v.sem_inc(cp_ev.sem, 2)
            v.sem_inc(a_pd.sem, 1)
            v.sem_inc(a_on.sem, 2)
            v.sem_inc(mg_ev.sem, 2)
            v.sem_inc(pq_s.sem, 2)
            v.sem_inc(dve_used.sem, len(V_DVE))
            v.sem_inc(pe_used.sem, len(V_PE))
            v.wait_ge(cst_in.sem, 7 * 16)
            v.sem_inc(layer_done.sem, 1)
            with v.Fori(0, DEPTH) as l:
                ppl = pp[:, :, :].rearrange("p l n -> p (l n)")
                rowl = row[:, :, :].rearrange("p l n -> p (l n)")

                def par(name, i=0, n=1):
                    return ppl[:, bass.ds(l * PPW + (PP[name][0] + i), n)]

                def rowp(o, n):
                    return rowl[:, bass.ds(l * (2 * HD + HEADS) + o, n)]

                v.wait_ge(w_used.sem, w_used.at(l, N_MOD))
                v.tensor_copy(AR.rearrange("p (b n) -> p b n", b=3), ps[:, 0:3, :]).then_inc(mod_ev.sem, 1)
                v.wait_ge(mod_t.sem, mod_t.at(l, 1))
                bada = par("bada", 0, 48).rearrange("p (q s h) -> p q h s", q=6, s=WS)
                ad5 = adaT[:, :, :].rearrange("p (q s h) c -> p q h s c", q=6, s=WS)
                for m in range(2 * N_MOD // WS):
                    src = ps[:, 4 + m // 4, (m % 4) * P:(m % 4 + 1) * P].rearrange("p (s c) -> p s c", s=WS)[:, :, 0:2]
                    v.tensor_tensor(out=ad5[:, m // 2, m % 2], in0=src,
                                    in1=bada[:, m // 2, m % 2].unsqueeze(2).broadcast_to([P, WS, 2]), op=ALU.add)
                v.drain()
                for kind in range(2):
                    gain = par(("n1", "n2")[kind], 0, KD)
                    for s in range(2):
                        v.scalar_tensor_tensor(out=aff[:, s, 2 * kind, :], in0=adaT[:, (1 + 3 * kind) * KD:(2 + 3 * kind) * KD, s],
                                               scalar=1.0, in1=gain, op0=ALU.add, op1=ALU.mult)
                        v.tensor_copy(aff[:, s, 2 * kind + 1, :], adaT[:, 3 * kind * KD:(3 * kind + 1) * KD, s])
                v.tensor_scalar(out=nsink[:, :], in0=rowp(2 * HD, HEADS), scalar1=-1.0, scalar2=None, op0=ALU.mult)\
                    .then_inc(aff_ok.sem, 1)
                for t in range(TILES):
                    square_sum(t)
                    v.drain()
                norm(l, 0)
                v.wait_ge(pads.sem, pads.at(l, 1))
                for j in range(CJ):
                    v.wait_ge(cp_sg.sem, cp_sg.at(l, j + 1))
                    bk = (j % 2) * 4
                    v.tensor_tensor(out=convh[:, j, PAD:PAD + P], in0=ps[:, bk + 1, 0:P], in1=G[:, j % 2, 0:P], op=ALU.mult)
                    v.tensor_tensor(out=convh[:, j, 3 * PAD + P:3 * PAD + TOK], in0=ps[:, bk, :], in1=G[:, j % 2, P:TOK],
                                    op=ALU.mult).then_inc(cp_ev.sem, 1)
                v.drain()
                for j in range(CJ):
                    v.tensor_scalar(out=YC[:, j, :], in0=convh[:, j, 0:SPAN], scalar1=par("cw", j * TAPS),
                                    scalar2=par("cb", j), op0=ALU.mult, op1=ALU.add)
                chf = M[:, 0:CJ * CPAD]
                with v.Fori(1, TAPS) as k:
                    v.drain()
                    for j in range(CJ):
                        v.scalar_tensor_tensor(out=YC[:, j, :], in0=chf[:, bass.ds(k + j * CPAD, SPAN)],
                                               scalar=ppl[:, bass.ds(l * PPW + k + (PP["cw"][0] + j * TAPS), 1)],
                                               in1=YC[:, j, :], op0=ALU.mult, op1=ALU.add)
                v.drain().then_inc(cv_y.sem, 1)
                v.wait_ge(qp_ev.sem, qp_ev.at(l, 5 * TILES))
                v.sem_inc(dve_go.sem, 1)
                tmf = A[:, 4352:10752]
                NH = HEADS + KVH

                def heads_of(t, lo=0, hi=NH):
                    return tmf[:, bass.ds(t * 1280 + lo * HD, (hi - lo) * HD)].rearrange("p (h d) -> p h d", d=HD)

                for t in range(TILES):
                    sq = T[:, :].rearrange("p (h d) -> p h d", d=HD)
                    v.tensor_tensor(out=sq, in0=heads_of(t), in1=heads_of(t), op=ALU.mult)
                    v.drain()
                    v.tensor_reduce(out=nrm[2][:, t * NH:(t + 1) * NH], in_=sq, axis=AX.X, op=ALU.add)
                    v.drain()
                v.tensor_scalar(out=nrm[0], in0=nrm[2], scalar1=1.0 / HD, scalar2=EPS, op0=ALU.mult, op1=ALU.add)\
                    .then_inc(kq_s.sem, 1)
                v.wait_ge(kq_r.sem, kq_r.at(l, 1))
                v.reciprocal(nrm[2], nrm[1])
                v.drain()
                for t in range(TILES):
                    v.tensor_tensor(out=heads_of(t), in0=heads_of(t),
                                    in1=nrm[2][:, t * NH:(t + 1) * NH].unsqueeze(2).broadcast_to([P, NH, HD]), op=ALU.mult)
                v.drain()
                for t in range(TILES):
                    for o, lo, hi in ((0, 0, HEADS), (HD, HEADS, NH)):
                        v.tensor_tensor(out=heads_of(t, lo, hi), in0=heads_of(t, lo, hi),
                                        in1=rowp(o, HD).unsqueeze(1).broadcast_to([P, hi - lo, HD]), op=ALU.mult)
                rpf = rope[:, :, :, :].rearrange("p c t d -> p (c t d)")
                with v.Fori(0, TILES - 1) as t:
                    for part in range(2):
                        heads = tmf[:, bass.ds(t * 1280 + (1280 + part * 640), 640)].rearrange("p (h d) -> p h d", d=HD)
                        sw = T[:, :].rearrange("p (h d) -> p h d", d=HD)
                        hd = HD // 2
                        v.drain()
                        for a, b in ((0, hd), (hd, 0)):
                            v.tensor_tensor(out=sw[:, :, a:a + hd], in0=heads[:, :, b:b + hd],
                                            in1=rpf[:, bass.ds(t * HD + (4 * HD + a), hd)].unsqueeze(1).broadcast_to([P, 10, hd]),
                                            op=ALU.mult)
                        v.drain()
                        v.tensor_tensor(out=heads, in0=heads,
                                        in1=rpf[:, bass.ds(t * HD, HD)].unsqueeze(1).broadcast_to([P, 10, HD]), op=ALU.mult)
                        v.drain()
                        v.tensor_tensor(out=heads, in0=heads, in1=sw, op=ALU.add)
                v.drain().then_inc(kq_ok.sem, 1)

                h = SPAN // 2
                v.wait_ge(ln_mp.sem, ln_mp.at(l, 1))
                for j in range(CJ):
                    y2 = YC[:, j, :].rearrange("p (b n) -> p b n", b=2)
                    last = v.tensor_tensor(out=y2, in0=y2, in1=ps[:, 2:4, 0:h], op=ALU.subtract)
                last.then_inc(ln_d.sem, 1)
                v.wait_ge(ln_vp.sem, ln_vp.at(l, 1))
                v.tensor_scalar(out=RSTD.rearrange("p (b n) -> p b n", b=2), in0=ps[:, 2:4, 0:h], scalar1=EPS, scalar2=None,
                                op0=ALU.add).then_inc(ln_v.sem, 1)
                v.wait_ge(ln_sr.sem, ln_sr.at(l, 1))
                v.reciprocal(RSTD, RSTD)
                v.drain()
                for j in range(CJ):
                    last = v.tensor_tensor(out=YC[:, j, :], in0=YC[:, j, :], in1=RSTD, op=ALU.mult)
                last.then_inc(ln_n.sem, 1)

                def attention(n, t):
                    u0 = n * UNITS
                    v.wait_ge(qt_ps.sem, qt_ps.at(l, n + 1))
                    v.tensor_copy(qT[:, 8:16, :], ps[0:HD, 2:4, :].rearrange("p b (u n) -> p (b u) n", n=P)).then_inc(qt_d.sem, 1)

                    def maxima(u):
                        bk, e = (u % 2) * 2, u % 2
                        nb = blocks(t, u)
                        v.wait_ge(a_s.sem, a_s.at(l, u0 + u + 1))
                        if nb == 5:
                            v.tensor_reduce(out=sm[:, 0, e:e + 1], in_=ps[:, bk:bk + 2, 0:HALF], axis=AX.XY, op=ALU.max)
                        else:
                            v.tensor_reduce(out=sm[:, 0, e:e + 1], in_=ps[:, bk, 0:nb * P], axis=AX.X, op=ALU.max)
                        v.drain()
                        if not windowed(u):
                            last = v.tensor_scalar(out=sm[:, 1, e:e + 1], in0=sm[:, 0, e:e + 1], scalar1=-SCALE, scalar2=None,
                                                   op0=ALU.mult)
                        else:
                            last = v.tensor_scalar(out=sm[:, 1, e:e + 1], in0=sm[:, 0, e:e + 1], scalar1=-SCALE,
                                                   scalar2=nsink[:, u:u + 1], op0=ALU.mult, op1=ALU.min)
                        last.then_inc(a_m.sem, 1)

                    def pt_copy(u):
                        w = dve_blocks(t, u) * P
                        e = u % 2
                        v.wait_ge(a_t.sem, a_t.at(l, u0 + u + 1))
                        if u >= 2:
                            v.wait_ge(a_o.sem, a_o.at(l, u0 + u - 1))
                        v.tensor_copy(PT[e][:, 0:w], ps[:, 4, 0:w]).then_inc(a_pd.sem, 1)
                        if windowed(u):
                            v.tensor_tensor(out=sm[:, 5, e:e + 1], in0=sm[:, 2, e:e + 1], in1=sm[:, 3, e:e + 1], op=ALU.add)
                            v.drain()
                            v.reciprocal(sm[:, 4, e:e + 1], sm[:, 5, e:e + 1])
                        else:
                            v.reciprocal(sm[:, 4, e:e + 1], sm[:, 2, e:e + 1])
                        v.drain()

                    def out(u):
                        v.wait_ge(a_o.sem, a_o.at(l, u0 + u + 1))
                        v.tensor_scalar(out=QO[:, u * HD:(u + 1) * HD], in0=ps[:, 6 + u % 2, 0:HD],
                                        scalar1=sm[:, 4, u % 2:u % 2 + 1], scalar2=None, op0=ALU.mult).then_inc(a_on.sem, 1)

                    for u in range(UNITS + 2):
                        if u < UNITS:
                            maxima(u)
                        else:
                            v.drain()
                        if 1 <= u <= UNITS:
                            pt_copy(u - 1)
                        if u >= 2:
                            out(u - 2)

                attention(0, None)
                with v.Fori(0, TILES - 1) as t:
                    attention(t + 1, t)

                for i in range(8):
                    if i:
                        v.wait_ge(rw_ps.sem, rw_ps.at(l, i))
                    j0 = (2 + 3 * (i // 4)) * KD + (i % 2) * 4
                    v.tensor_tensor(out=T[:, 0:512].rearrange("p (j n) -> p j n", j=4),
                                    in0=ident.unsqueeze(1).broadcast_to([P, 4, P]),
                                    in1=adaT[:, j0:j0 + 4, (i // 2) % 2].unsqueeze(2).broadcast_to([P, 4, P]),
                                    op=ALU.mult).then_inc(rw_dg.sem, 1)
                mf = M[:, :]
                with v.Fori(0, KD) as j:
                    for b in range(4):
                        v.wait_ge(mg_sg.sem, mg_sg.at(l, j * 4 + b + 1))
                        v.wait_ge(w_used.sem, w_used.at(l, j * 4 + (b + AT_MG + 1)))
                        bk = (b % 2) * 4 + 2
                        dst = mf[:, bass.ds(j * TOK, TOK)]
                        to = dst if b == 0 else PR
                        v.tensor_tensor(out=to.rearrange("p (b n) -> p b n", b=2), in0=ps[:, bk:bk + 2, 0:HALF],
                                        in1=SG[b % 2].rearrange("p (b n) -> p b n", b=2), op=ALU.mult).then_inc(mg_ev.sem, 1)
                        v.drain()
                        if b:
                            v.tensor_tensor(out=dst, in0=dst, in1=PR, op=ALU.add)
                            last = v.drain()
                    last.then_inc(mg_m.sem, 1)
                for t in range(TILES):
                    bk = (t % 4) * 2
                    if t < TILES - 1:
                        v.wait_ge(op_ps.sem, op_ps.at(l, t + 1))
                    else:
                        v.wait_ge(w_used.sem, w_used.at(l, AT_PQ))
                    v.tensor_tensor(out=JX.rearrange("p (b n) -> p b n", b=2), in0=ps[:, bk:bk + 2, :],
                                    in1=grow[:, 0, min(t, 1), :].rearrange("p (b n) -> p b n", b=2), op=ALU.mult).then_inc(op_x.sem, 1)
                    v.drain()
                    v.tensor_tensor(out=x[:, t, :], in0=x[:, t, :], in1=JX, op=ALU.add)
                    v.drain()
                    square_sum(t)
                    v.drain()
                norm(l, TILES)
                def top16(values, val, idx):
                    rows = range(len(values))
                    for r in rows:
                        v.max(val[r][:, 0:8], values[r])
                    v.drain()
                    for r in rows:
                        v.max_index(idx[r][:, 0:8], val[r][:, 0:8], values[r])
                    v.drain()
                    for r in rows:
                        v.match_replace(values[r], val[r][:, 0:8], values[r], -3e38)
                    v.drain()
                    for r in rows:
                        v.max(val[r][:, 8:16], values[r])
                    v.drain()
                    for r in rows:
                        v.max_index(idx[r][:, 8:16], val[r][:, 8:16], values[r])
                    v.drain()

                def best_experts(w, t, h):
                    v.tensor_copy(w.hs, A[:, bass.ds(t * (UNITS * P) + h * (2 * P), 2 * P)])
                    v.drain()
                    top16([w.hs[:, 0:P], w.hs[:, P:2 * P]], [w.sv[:, c, :] for c in range(2)], [w.si[:, c, :] for c in range(2)])
                    v.tensor_copy(w.sf, w.si)
                    v.tensor_tensor(out=w.cand.rearrange("p (a b) -> p a b", a=TOPK),
                                    in0=w.sv[:, 0, :].unsqueeze(2).broadcast_to([P, TOPK, TOPK]),
                                    in1=w.sv[:, 1, :].unsqueeze(1).broadcast_to([P, TOPK, TOPK]), op=ALU.add)
                    v.drain()
                    top16([w.cand], [w.tv], [w.ti])
                    v.tensor_scalar(out=GT[:, bass.ds(t * SLOTS + h * TOPK, TOPK)], in0=w.tv, scalar1=w.tv[:, 0:1], scalar2=None,
                                    op0=ALU.subtract)
                    v.tensor_scalar(out=w.pu[:, 0, :], in0=w.ti, scalar1=TOPK * (TOPK - 1), scalar2=None, op0=ALU.bitwise_and)
                    v.tensor_scalar(out=w.pu[:, 1, :], in0=w.ti, scalar1=TOPK - 1, scalar2=None, op0=ALU.bitwise_and)
                    v.drain()
                    v.tensor_copy(w.pf, w.pu)
                    v.drain()
                    full = [P, 2, TOPK, TOPK]
                    v.tensor_tensor(out=w.EQ, in0=w.pf.unsqueeze(3).broadcast_to(full),
                                    in1=io[:, 0:2 * TOPK].rearrange("p (c a) -> p c a", c=2).unsqueeze(2).broadcast_to(full),
                                    op=ALU.is_equal)
                    v.drain()
                    v.tensor_tensor(out=w.EQ, in0=w.EQ, in1=w.sf.unsqueeze(2).broadcast_to(full), op=ALU.mult)
                    v.drain()
                    v.tensor_reduce(out=w.ef, in_=w.EQ, axis=AX.X, op=ALU.add)
                    v.drain()
                    v.scalar_tensor_tensor(out=w.er, in0=w.ef[:, 0, :], scalar=float(P), in1=w.ef[:, 1, :], op0=ALU.mult, op1=ALU.add)
                    v.drain()
                    v.tensor_scalar(out=EI[:, bass.ds(t * SLOTS + h * TOPK, TOPK)], in0=w.er,
                                    scalar1=io[:, bass.ds(l + 2 * TOPK, 1)], scalar2=None, op0=ALU.add)
                    v.drain().then_inc(ei_ok.sem, 1)

                v.wait_ge(nk_done.sem, nk_done.at(l, 64))
                v.sem_inc(dve_go.sem, 1)
                scf = A[:, 0:10240].rearrange("p (t n) -> p t n", t=TILES)
                with v.Fori(0, PH) as h:
                    for i in range(2):
                        hp = h * 2 + i
                        v.wait_ge(pq_sp.sem, pq_sp.at(l, hp + 1))
                        v.tensor_copy(scf[:, 0:4, bass.ds(hp * P, P)], ps[:, 2 * i, :].rearrange("p (t n) -> p t n", n=P))
                        v.tensor_copy(scf[:, 4, bass.ds(hp * P, P)], ps[:, 2 * i + 1, 0:P]).then_inc(pq_s.sem, 1)
                    v.drain()
                    best_experts(early, 0, h)
                v.drain().then_inc(early_ok.sem, 1)

                def group_products(t, g):
                    for b in range(RING):
                        v.wait_ge(got[b].sem, got[b].at(l, (t * 2 * GROUPS + g + 1) * 16))
                        v.wait_ge(dve_used.sem, dve_used.at(l, t * DVE_TILE + g * RING + (b - 1)))
                        v.scalar_tensor_tensor(out=junk[b % 2], in0=ring[b], scalar=1.0, in1=M[:, bass.ds(t * D, D)],
                                               op0=ALU.mult, op1=ALU.mult, accum_out=dots[:, bass.ds(g * RING + b, 1)])\
                            .then_inc(dve_used.sem, 1)

                def weights(t):
                    v.drain().then_inc(u_done.sem, 1)
                    v.wait_ge(u_act.sem, u_act.at(l, t + 1))
                    e3 = ew.rearrange("p (h k) -> p h k", h=PH)
                    v.tensor_tensor(out=wgt, in0=dots, in1=ew, op=ALU.mult)
                    v.tensor_reduce(out=s1[:, 0:8], in_=e3, axis=AX.X, op=ALU.add)
                    for a in acc:
                        v.memset(a, 0.0)
                    v.drain()
                    v.reciprocal(s1[:, 8:16], s1[:, 0:8])
                    v.drain()
                    w3 = wgt.rearrange("p (h k) -> p h k", h=PH)
                    v.tensor_tensor(out=w3, in0=w3, in1=s1[:, 8:16].unsqueeze(2).broadcast_to([P, PH, TOPK]), op=ALU.mult)
                    v.drain().then_inc(wgt_ok.sem, 1)

                def group_sums(t, g):
                    for i, b in enumerate(V_DVE):
                        v.wait_ge(got[b].sem, got[b].at(l, (t * 2 * GROUPS + GROUPS + g + 1) * 16))
                        v.wait_ge(dve_used.sem, dve_used.at(l, t * DVE_TILE + g * len(V_DVE) + (DVE_U + i - 1)))
                        v.scalar_tensor_tensor(out=acc[i % 2], in0=ring[b], scalar=wgt[:, bass.ds(g * RING + b, 1)],
                                               in1=acc[i % 2], op0=ALU.mult, op1=ALU.add).then_inc(dve_used.sem, 1)

                def residual(t, s):
                    v.drain()
                    v.tensor_tensor(out=acc[0], in0=acc[0], in1=acc[1], op=ALU.add)
                    v.drain()
                    v.wait_ge(pe_used.sem, pe_used.at(l, (t + 1) * PE_TILE))
                    a2 = acc[0].rearrange("p (b n) -> p b n", b=2)
                    v.tensor_tensor(out=a2, in0=a2, in1=ps[:, 6:8, :], op=ALU.add)
                    v.drain()
                    v.tensor_tensor(out=acc[0], in0=acc[0], in1=grow[:, 1, s, :], op=ALU.mult)
                    v.drain()
                    xt = xf[:, bass.ds(t * D, D)]
                    v.tensor_tensor(out=xt, in0=xt, in1=acc[0], op=ALU.add)
                    v.drain()

                def tile(t, s, more):
                    with v.Fori(0, GROUPS) as g:
                        group_products(t, g)
                    weights(t)
                    with v.Fori(0, GROUPS) as g:
                        group_sums(t, g)
                        if more:
                            best_experts(steady, t + 1, g)
                    residual(t, s)

                tile(0, 0, True)
                with v.Fori(1, TILES - 1) as t:
                    tile(t, 1, True)
                tile(TILES - 1, 1, False)
                v.drain().then_inc(layer_done.sem, 1)

            v.wait_ge(f_g.sem, 16)
            for t in range(TILES):
                square_sum(t)
                v.drain()
            inverse_roots(f_ss, f_sq, 1)
            for t in range(TILES):
                v.scalar_tensor_tensor(out=h2[:, t, :], in0=x[:, t, :], scalar=s1[:, 3 * TILES + t:3 * TILES + t + 1],
                                       in1=R[:, 0:D], op0=ALU.mult, op1=ALU.mult).then_inc(f_y.sem, 1)


def windowed(u):
    return u < HEADS


def blocks(t, u):
    return 1 if t is None else 4 if windowed(u) else 5


def dve_blocks(t, u):
    return (blocks(t, u) + 1) // 2


def shape_constants():
    f8 = np.float64
    eye = np.eye(P, dtype=np.float32)
    ones = np.full((P, P), 1.0 / CONV, np.float32)

    def dft(n):
        a = 2 * np.pi * ((np.arange(n)[:, None] * np.arange(n)[None, :]) % n).astype(f8) / n
        return np.cos(a) / np.sqrt(n), np.sin(a) / np.sqrt(n)

    c64, s64 = dft(HD)
    z = np.zeros((HD, HD))
    bc, bs = np.block([[c64, z], [z, c64]]), -np.block([[s64, z], [z, s64]])
    c1, s1 = dft(P)
    nf = HD // 4
    inv = (1.0 / (np.float32(10000.0) ** (np.arange(nf, dtype=np.float32) / np.float32(nf)))).astype(np.float32)
    pos = np.arange(LAT)
    ang = np.concatenate([(pos // 64).astype(np.float32)[:, None] * inv, (pos % 64).astype(np.float32)[:, None] * inv], -1)
    c, s = np.cos(ang), np.sin(ang)
    cc, ss = np.concatenate([c, c], -1), np.concatenate([-s, s], -1)
    rope = np.stack([cc, ss]).reshape(2, 4, P, HD).transpose(2, 0, 1, 3).reshape(P, -1)
    io = np.concatenate([np.arange(TOPK) * TOPK, np.arange(TOPK), np.arange(DEPTH) * EXPERTS])
    io = np.broadcast_to(io, (P, io.size))
    cst = np.concatenate([eye, ones, bc, bs, rope, io], 1).astype(np.float32)
    tab = np.concatenate([m.reshape(4, P, LAT).transpose(1, 0, 2).reshape(P, -1) for m in dft(LAT)] + [c1, s1], 1)
    tab = tab.astype(np.float32)
    q, k = np.arange(P)[:, None], np.arange(P)[None, :]
    lo, up, no = np.where(k >= q, 0, NEG), np.where(k <= q, 0, NEG), np.full((P, P), NEG)
    mask = np.concatenate([m for t in range(4) for m in (no if t == 0 else lo, no if t == 3 else up)], 1).astype(np.float32)
    return cst, tab, mask


def kernel(**inp):
    import concourse.bacc as bacc
    from concourse.bass_utils import run_bass_kernel_spmd as run

    g = {k: np.asarray(v) for k, v in inp.items()}

    def cols(w, width=256):
        d, k, n = w.shape
        return w.reshape(d, k // P, P, n // width, width).transpose(0, 3, 2, 1, 4).reshape(d, n // width, P, -1)

    w_in = g["w_in"]
    f, c_a, c_g, aq, ak, av, wq, wk, wv, gl = np.split(
        w_in, np.cumsum([512, 512, 512, 512, 128, 128, 512, 128, 128]), axis=2)
    conv = np.stack([c_a.reshape(DEPTH, D, CJ, P), c_g.reshape(DEPTH, D, CJ, P)], 3).reshape(DEPTH, D, 1024)
    branch = [g["w_fourier_out"], g["w_conv_out"], g["w_attn_out"], g["w_win_out"]]
    merge = []
    for b in range(4):
        gates = cols(gl[:, :, b * D:(b + 1) * D], P)
        merge.append(np.concatenate([gates, cols(branch[b], P), np.zeros((DEPTH, KD, P, 512), np.float32)], 3))
    merge = np.stack(merge, 2).reshape(DEPTH, N_MG, P, SLOT_W)
    ws = np.concatenate([cols(g["w_ada"]), cols(conv), cols(aq), cols(wq), cols(np.concatenate([ak, wk, av, wv], 2)), cols(f),
                         merge, cols(g["w_out"]), cols(g["w_peer_q"])], 1).reshape(DEPTH * LOADS * P, SLOT_W)

    def pt(a):
        return a.reshape(DEPTH, -1, P).transpose(2, 0, 1)

    cw = g["conv_dw"].reshape(DEPTH, TAPS, CJ, P).transpose(3, 0, 2, 1).reshape(P, DEPTH, -1)
    ppd = np.concatenate([pt(g["norm1_g"]), pt(g["norm2_g"]), pt(g["b_ada"]), pt(g["b_gate"].reshape(DEPTH, -1)), cw,
                          pt(g["conv_b"]), pt(g["conv_ln_g"]), pt(g["conv_ln_b"])], 2).reshape(P, -1)
    cvec = np.stack([g["c_ctx"], g["c"][0]], 1).reshape(KD, P, 2).transpose(1, 0, 2).reshape(P, -1)
    rowd = np.concatenate([g["q_norm_g"], g["k_norm_g"], g["win_sink"]], 1)
    skd = g["peer_subkeys"].transpose(0, 3, 1, 2).reshape(DEPTH * P, 2 * P)
    kcd = np.stack([g["cache_attn_k"][0], g["cache_win_k"][0]], 1).transpose(0, 1, 4, 3, 2).reshape(DEPTH * 2 * HD, KVH * P)
    vcd = np.concatenate([g["cache_attn_v"][0].reshape(DEPTH * P, P), g["cache_win_v"][0].reshape(DEPTH * P, P)], 1)
    xin = np.concatenate([g["x_prompt"][0], g["x_sample"][0]], 0)
    cst, tab, mask = shape_constants()
    arrays = dict(ws=ws, cst=cst, tabs=tab, masks=mask, ppd=ppd, cvec=cvec, rowd=rowd, fing=g["final_norm_g"], skd=skd,
                  kcd=kcd, vcd=vcd, tables_u=g["peer_u"].reshape(-1, D), tables_v=g["peer_v"].reshape(-1, D), xin=xin)
    arrays = {k: np.ascontiguousarray(a) for k, a in arrays.items()}
    nc = bacc.Bacc("TRN2", target_bir_lowering=False, num_devices=1)
    args = [nc.dram_tensor(k, a.shape, F32, kind="ExternalInput").ap() for k, a in arrays.items()]
    y = nc.dram_tensor("y", (TOK, D), F32, kind="ExternalOutput").ap()
    nk = nc.dram_tensor("nk", (4 * DEPTH * P, P), F32, kind="ExternalOutput").ap()
    program(nc, *args, y, nk)
    r = run(nc, [arrays], core_ids=[0]).results[0]
    y, nk = r["y"], r["nk"].reshape(4, 1, DEPTH, P, KVH, HD)
    return y[None, :P], y[None, P:], nk[0], nk[1], nk[2], nk[3]
```
